# Optimizing a Trainium2 kernel written in Bass

```python
import jax, jax.numpy as jnp
from jax import lax
import numpy as np

D_MODEL = 1024
BATCH = 1
SEQ = 128
DEPTH = 1
DEC_BATCH = 1
DEC_SEQ = 512
PAST_LEN = 128

GRID_W = 64
GLA_HEADS = 4
GLA_DK = D_MODEL // 16
GLA_DV = D_MODEL // 8
GLA_WIDTH = GLA_HEADS * GLA_DV
GATE_RANK = 16
GATE_NORM = 16.0
CHUNK = 64
POOL_WINDOWS = (2, 4, 8, 16)
POOL_GROUPS = 4
POOL_WIDTH = D_MODEL // 2
POOL_GC = POOL_WIDTH // POOL_GROUPS
MIX_WIDTH = GLA_WIDTH + POOL_WIDTH
N_EXPERTS = 16
CAPACITY_FACTOR = 2
D_FF_EXPERT = ((8 * D_MODEL // 3 + 127) // 128) * 128
SPLITS = (GLA_HEADS * GLA_DK, GLA_HEADS * GLA_DK, GLA_WIDTH, GLA_WIDTH, GATE_RANK, GATE_RANK, POOL_WIDTH)
IN_COLS = sum(SPLITS)
EPS = 1e-6

kernel_name = "hybrid_gla_pool_ecmoe_diffusion_step"

def rmsnorm(x, g):
    xf = x.astype(jnp.float32)
    y = xf * lax.rsqrt(jnp.mean(xf * xf, axis=-1, keepdims=True) + EPS)
    return (y * g.astype(jnp.float32)).astype(x.dtype)

def grid_pos_embed(L, dtype):
    rows = L // GRID_W
    row = jnp.repeat(jnp.arange(rows), GRID_W).astype(jnp.float32)
    col = jnp.tile(jnp.arange(GRID_W), rows).astype(jnp.float32)
    quarter = D_MODEL // 4
    omega = 1.0 / (10000.0 ** (jnp.arange(quarter, dtype=jnp.float32) / quarter))
    er = row[:, None] * omega[None, :]
    ec = col[:, None] * omega[None, :]
    return jnp.concatenate([jnp.sin(er), jnp.cos(er), jnp.sin(ec), jnp.cos(ec)], axis=-1).astype(dtype)

def gla_chunked(q, k, v, log_a, s0):
    B, H, L, DK = q.shape
    DV = v.shape[-1]
    N = L // CHUNK
    q = q.reshape(B, H, N, CHUNK, DK)
    k = k.reshape(B, H, N, CHUNK, DK)
    v = v.reshape(B, H, N, CHUNK, DV)
    b = jnp.cumsum(log_a.reshape(B, H, N, CHUNK, DK), axis=3)
    b_last = b[:, :, :, -1:, :]
    q_dec = q * jnp.exp(b)
    k_intra = k * jnp.exp(-b)
    k_state = k * jnp.exp(b_last - b)
    mask = jnp.tril(jnp.ones((CHUNK, CHUNK), dtype=bool))
    attn = jnp.where(mask, jnp.einsum("bhncd,bhnsd->bhncs", q_dec, k_intra), 0.0)
    o_intra = jnp.einsum("bhncs,bhnsv->bhncv", attn, v)
    chunk_kv = jnp.einsum("bhncd,bhncv->bhndv", k_state, v)
    decay = jnp.exp(b_last[:, :, :, 0, :])

    def step(s, inp):
        dec, kv = inp
        return dec[..., None] * s + kv, s

    s_final, s_starts = lax.scan(step, s0, (jnp.moveaxis(decay, 2, 0), jnp.moveaxis(chunk_kv, 2, 0)))
    o_inter = jnp.einsum("bhncd,nbhdv->bhncv", q_dec, s_starts)
    return (o_intra + o_inter).reshape(B, H, L, DV), s_final

def multiscale_pool(u, seg_len):
    B, L, _ = u.shape
    uf = u.astype(jnp.float32)
    cs = jnp.concatenate([jnp.zeros((B, 1, POOL_WIDTH), jnp.float32), jnp.cumsum(uf, axis=1)], axis=1)
    t = jnp.arange(L)
    seg_start = (t // seg_len) * seg_len
    seg_end = seg_start + seg_len - 1
    outs = []
    for gi, w in enumerate(POOL_WINDOWS):
        sl = slice(gi * POOL_GC, (gi + 1) * POOL_GC)
        lo = jnp.maximum(t - w // 2, seg_start)
        hi = jnp.minimum(t - w // 2 + w - 1, seg_end)
        csg = cs[:, :, sl]
        s = csg[:, hi + 1] - csg[:, lo]
        cnt = (hi - lo + 1).astype(jnp.float32)
        outs.append(s / cnt[None, :, None] - uf[:, :, sl])
    return jnp.stack(outs, axis=2)

def token_mixer(h, lp, s0_f, s0_b, seg_len):
    B, L, _ = h.shape
    f32 = jnp.float32
    proj = h @ lp["w_in"]
    offs, acc = [], 0
    for n in SPLITS[:-1]:
        acc += n
        offs.append(acc)
    q, k, v, g, za_f, za_b, u = jnp.split(proj, offs, axis=-1)

    def heads(t, d):
        return t.astype(f32).reshape(B, L, GLA_HEADS, d).transpose(0, 2, 1, 3)

    qh = heads(q, GLA_DK) * (GLA_DK ** -0.5)
    kh = heads(k, GLA_DK)
    vh = heads(v, GLA_DV)
    la_f = heads(jax.nn.log_sigmoid((za_f @ lp["w_a_up_f"] + lp["b_a_f"]).astype(f32)), GLA_DK) / GATE_NORM
    la_b = heads(jax.nn.log_sigmoid((za_b @ lp["w_a_up_b"] + lp["b_a_b"]).astype(f32)), GLA_DK) / GATE_NORM
    rev = lambda t: jnp.flip(t, axis=2)
    o_f, s_f = gla_chunked(qh, kh, vh, la_f, s0_f)
    o_b, s_b = gla_chunked(rev(qh), rev(kh), rev(vh), rev(la_b), s0_b)
    o = o_f + rev(o_b)
    o = o * lax.rsqrt(jnp.mean(o * o, axis=-1, keepdims=True) + EPS) * lp["gla_norm_g"].astype(f32)
    o = o.transpose(0, 2, 1, 3).reshape(B, L, GLA_WIDTH) * jax.nn.silu(g.astype(f32))

    p = multiscale_pool(u, seg_len)
    pool_out = jnp.einsum("blgc,gcd->blgd", p, lp["w_pool"].astype(f32)).reshape(B, L, POOL_WIDTH)
    pool_out = pool_out * lp["pool_scale"].astype(f32)

    y = jnp.concatenate([o, pool_out], axis=-1).astype(h.dtype) @ lp["w_out"]
    return y, s_f, s_b

def ec_moe(h, lp):
    B, L, D = h.shape
    n = B * L
    xf = h.reshape(n, D)
    probs = jax.nn.softmax((xf @ lp["w_router"]).astype(jnp.float32), axis=-1)
    cap = CAPACITY_FACTOR * n // N_EXPERTS
    gate_vals, tok_idx = lax.top_k(probs.T, cap)
    xe = jnp.take(xf, tok_idx, axis=0)
    hid = jax.nn.silu(jnp.einsum("ecd,edf->ecf", xe, lp["w_e_gate"])) * jnp.einsum("ecd,edf->ecf", xe, lp["w_e_up"])
    ye = jnp.einsum("ecf,efd->ecd", hid, lp["w_e_down"]) * gate_vals[..., None].astype(h.dtype)
    y = jnp.zeros_like(xf).at[tok_idx.reshape(-1)].add(ye.reshape(-1, D))
    return y.reshape(B, L, D)

def trunk_layer(x, cond, lp, s0_f, s0_b, seg_len):
    mod = jax.nn.silu(cond) @ lp["w_ada"] + lp["b_ada"]
    shift_a, scale_a, gate_a, shift_f, scale_f, gate_f = jnp.split(mod.astype(x.dtype), 6, axis=-1)
    h = rmsnorm(x, lp["norm_mix_g"]) * (1 + scale_a) + shift_a
    y, s_f, s_b = token_mixer(h, lp, s0_f, s0_b, seg_len)
    x = x + gate_a * y
    h = rmsnorm(x, lp["norm_ffn_g"]) * (1 + scale_f) + shift_f
    x = x + gate_f * ec_moe(h, lp)
    return x, s_f, s_b

def setup_inputs(seed: int = 0) -> dict:
    key = jax.random.key(seed)
    ks = jax.random.split(key, 24)
    f32 = jnp.float32
    D = D_MODEL
    nrm = lambda k, shape, s: jax.random.normal(k, shape, f32) * s
    st_shape = (DEC_BATCH, DEPTH, GLA_HEADS, GLA_DK, GLA_DV)
    return {
        "x_prompt": nrm(ks[0], (BATCH, SEQ, D), 1.0),
        "x_sample": nrm(ks[1], (DEC_BATCH, DEC_SEQ, D), 1.0),
        "state_gla_fwd": nrm(ks[2], st_shape, 1.0),
        "state_gla_bwd": nrm(ks[3], st_shape, 1.0),
        "c": nrm(ks[4], (DEC_BATCH, D), 1.0),
        "c_ctx": nrm(ks[5], (D,), 1.0),
        "norm_mix_g": 1.0 + nrm(ks[6], (DEPTH, D), 0.02),
        "w_ada": nrm(ks[7], (DEPTH, D, 6 * D), 0.5 * D ** -0.5),
        "b_ada": nrm(ks[8], (DEPTH, 6 * D), 0.02),
        "w_in": nrm(ks[9], (DEPTH, D, IN_COLS), D ** -0.5),
        "w_a_up_f": nrm(ks[10], (DEPTH, GATE_RANK, GLA_HEADS * GLA_DK), GATE_RANK ** -0.5),
        "b_a_f": nrm(ks[11], (DEPTH, GLA_HEADS * GLA_DK), 0.1),
        "w_a_up_b": nrm(ks[12], (DEPTH, GATE_RANK, GLA_HEADS * GLA_DK), GATE_RANK ** -0.5),
        "b_a_b": nrm(ks[13], (DEPTH, GLA_HEADS * GLA_DK), 0.1),
        "gla_norm_g": 1.0 + nrm(ks[14], (DEPTH, GLA_DV), 0.02),
        "w_pool": nrm(ks[15], (DEPTH, POOL_GROUPS, POOL_GC, POOL_GC), POOL_GC ** -0.5),
        "pool_scale": 1.0 + nrm(ks[16], (DEPTH, POOL_WIDTH), 0.1),
        "w_out": nrm(ks[17], (DEPTH, MIX_WIDTH, D), MIX_WIDTH ** -0.5),
        "norm_ffn_g": 1.0 + nrm(ks[18], (DEPTH, D), 0.02),
        "w_router": nrm(ks[19], (DEPTH, D, N_EXPERTS), D ** -0.5),
        "w_e_gate": nrm(ks[20], (DEPTH, N_EXPERTS, D, D_FF_EXPERT), D ** -0.5),
        "w_e_up": nrm(ks[21], (DEPTH, N_EXPERTS, D, D_FF_EXPERT), D ** -0.5),
        "w_e_down": nrm(ks[22], (DEPTH, N_EXPERTS, D_FF_EXPERT, D), D_FF_EXPERT ** -0.5),
        "final_norm_g": 1.0 + nrm(ks[23], (D,), 0.02),
    }

def reference(x_prompt, x_sample, state_gla_fwd, state_gla_bwd, c, c_ctx, norm_mix_g, w_ada, b_ada,
              w_in, w_a_up_f, b_a_f, w_a_up_b, b_a_b, gla_norm_g, w_pool, pool_scale, w_out,
              norm_ffn_g, w_router, w_e_gate, w_e_up, w_e_down, final_norm_g):
    def layer_params(l):
        return {"norm_mix_g": norm_mix_g[l], "w_ada": w_ada[l], "b_ada": b_ada[l], "w_in": w_in[l],
                "w_a_up_f": w_a_up_f[l], "b_a_f": b_a_f[l], "w_a_up_b": w_a_up_b[l], "b_a_b": b_a_b[l],
                "gla_norm_g": gla_norm_g[l], "w_pool": w_pool[l], "pool_scale": pool_scale[l],
                "w_out": w_out[l], "norm_ffn_g": norm_ffn_g[l], "w_router": w_router[l],
                "w_e_gate": w_e_gate[l], "w_e_up": w_e_up[l], "w_e_down": w_e_down[l]}

    xc = x_prompt
    Bp, Lc, _ = xc.shape
    cond_ctx = c_ctx[None, None, :]
    new_f, new_b = [], []
    for l in range(DEPTH):
        zero_state = jnp.zeros((Bp, GLA_HEADS, GLA_DK, GLA_DV), jnp.float32)
        xc, s_f, s_b = trunk_layer(xc, cond_ctx, layer_params(l), zero_state, zero_state, Lc)
        new_f.append(s_f)
        new_b.append(s_b)
    y_prompt = rmsnorm(xc, final_norm_g)
    new_state_gla_fwd = jnp.stack(new_f, axis=1)
    new_state_gla_bwd = jnp.stack(new_b, axis=1)

    Ls = x_sample.shape[1]
    xs = x_sample + grid_pos_embed(Ls, x_sample.dtype)[None]
    cond_lat = c[:, None, :]
    for l in range(DEPTH):
        s0_f = state_gla_fwd[:, l].astype(jnp.float32)
        s0_b = state_gla_bwd[:, l].astype(jnp.float32)
        xs, _, _ = trunk_layer(xs, cond_lat, layer_params(l), s0_f, s0_b, GRID_W)
    y_sample = rmsnorm(xs, final_norm_g)

    return (y_prompt, y_sample, new_state_gla_fwd, new_state_gla_bwd)


_drawn_inputs = setup_inputs


def setup_inputs(seed=0):
    import zlib

    import numpy as np

    out = dict(_drawn_inputs(seed))
    spreads = {}
    factors = {'state_gla_fwd': 8.0,
     'state_gla_bwd': 8.0,
     'gla_norm_g': 8.0,
     'norm_ffn_g': 8.0,
     'final_norm_g': 2.905}
    for name, (base, spread) in spreads.items():
        noise = np.random.default_rng([zlib.crc32(name.encode()), seed]).standard_normal(out[name].shape)
        drawn = base * np.exp(spread * noise) if base else spread * noise
        out[name] = __import__('jax').numpy.asarray(drawn.astype(out[name].dtype))
    for name, factor in factors.items():
        out[name] = (out[name] * factor).astype(out[name].dtype)
    return out
```

```python
from contextlib import ExitStack

import concourse.bass as bass
from concourse import mybir

F32 = mybir.dt.float32
F32R = mybir.dt.float32r
U32 = mybir.dt.uint32
ALU = mybir.AluOpType
ACT = mybir.ActivationFunctionType
AX_X = mybir.AxisListType.X

P = 128
D = 1024
KD = D // P
L_LAT, L_CTX = 512, 128
T_LAT = L_LAT // P
TILES = T_LAT + 1
NTOK = L_LAT + L_CTX
LAT, CTX = 0, 1
HEADS, DK, DV, CHUNK = 4, 64, 128, 64
HP = HEADS // 2
RANK = 16
POOLS = (2, 4, 8, 16)
GRID_W = 64
EXPERTS = 16
FF = 2816
CAP_LAT, CAP_CTX = 2 * L_LAT // EXPERTS, 2 * L_CTX // EXPERTS
SLOTS = CAP_LAT + CAP_CTX
EPS = 1e-6

UNIT = 2048
RING = 11
PRE_RING = 3
SPLIT = 3
GROUP = 256
GROUPS = FF // GROUP
EXP_UNITS = 3 * GROUPS
assert EXP_UNITS % RING == 0 and EXP_UNITS % SPLIT == 0

ADA_FIRST = 4
ADA_BLOCKS = 6 * D // 512
PRE = [("ada", b, kh) for b in range(ADA_FIRST) for kh in range(2)]
WIN_BLOCKS = (0, 512, 1568, 1024)
WIN0 = len(PRE)
PRE += [("win", b, kh) for b in range(4) for kh in range(2)]
ADA0 = len(PRE)
PRE += [("ada", b, kh) for b in range(ADA_FIRST, ADA_BLOCKS) for kh in range(2)]
WOUT0 = len(PRE)
PRE += [("wout", b, kh) for b in range(2) for kh in range(2)]
NPRE = len(PRE)
assert NPRE % PRE_RING == 0 and NPRE % SPLIT == 0

V_C, V_CCTX, V_BADA, V_GMIX, V_GFFN, V_GGLA, V_PSC, V_ROWS = 0, 8, 16, 64, 72, 80, 81, 85
K_ID, K_TRIF, K_TRIB, K_POOL, K_SEL, K_COLS = 0, 128, 256, 384, 384 + 8 * 128, 384 + 8 * 128 + 3 * 128


def expert_units():
    order = [("gate", 0), ("up", 0)]
    for g in range(1, GROUPS):
        order += [("gate", g), ("up", g), ("down", g - 1)]
    return order + [("down", GROUPS - 1)]


UNITS = expert_units()
AT = {u: j for j, u in enumerate(UNITS)}


def state_slot(t, c, direction, start):
    first = (0, 9)[direction] if t < T_LAT else (18, 21)[direction]
    n = (2 * t if t < T_LAT else 0) + c
    return first + (n + (direction == 1) if start else n + (direction == 0))


def build(nc, x_prompt, x_sample, state_fwd, state_bwd, c, c_ctx, norm_mix_g, w_ada, b_ada, w_in,
          w_a_up_f, b_a_f, w_a_up_b, b_a_b, gla_norm_g, w_pool, pool_scale, w_out, norm_ffn_g,
          w_router, w_e_gate, w_e_up, w_e_down, final_norm_g, consts, pos, y_prompt, y_sample,
          out_fwd, out_bwd):
    ctx = ExitStack()
    with ctx:
        base = (nc.sbuf_base + 63) // 64 * 64
        KB = 1024
        RAW = base
        HT = RAW + PRE_RING * UNIT * 4
        ST = HT + 40 * KB
        SPL = RAW + RING * UNIT * 4
        DR = SPL + 2 * SPLIT * UNIT * 4
        EX = DR + 40 * KB

        def at(name, shape, dt, offset):
            return nc.alloc_sbuf_tensor_at(name, shape, dt, offset=offset)

        raw = at("raw", [P, RING, UNIT], F32, RAW)
        w_hi = at("w_hi", [P, SPLIT, UNIT], F32R, SPL)
        w_lo = at("w_lo", [P, SPLIT, UNIT], F32R, SPL + SPLIT * UNIT * 4)

        here = [EX]

        def keep(name, shape, dt=F32):
            size = 4
            for n in shape[1:]:
                size *= n
            t = at(name, shape, dt, here[0])
            here[0] += (size + 31) // 32 * 32
            return t

        const = keep("const", [P, K_COLS])
        cond = keep("cond", [P, KD, P], F32R)
        wpool = keep("wpool", [P, 4, P])
        wrt = keep("wrt", [P, KD, EXPERTS])
        vecT = keep("vecT", [P, V_ROWS])
        silu_c = keep("silu_c", [P, 16])
        modT = keep("modT", [P, 48, 2])
        modP = keep("modP", [P, 4, 2])
        scaleA = keep("scaleA", [P, KD, 2])
        scaleF = keep("scaleF", [P, KD, 2])
        eps = keep("eps", [P, 1])
        ss = keep("ss", [P, 20])
        rstd = keep("rstd", [P, 20])
        dec = keep("dec", [P, TILES, 2, HP, 2])
        modrow = keep("modrow", [5, 2, 512])
        wza = keep("wza", [P, KD, 2 * RANK])
        late = here[0]
        wup = keep("wup", [2 * RANK + 1, 512])
        la = keep("la", [P, TILES, 512])
        assert here[0] <= nc.sbuf_usable_end, (here[0], nc.sbuf_usable_end)
        wza_hi = at("wza_hi", [P, KD, SLOTS], F32R, late + 2 * KB)
        wza_lo = at("wza_lo", [P, KD, SLOTS], F32R, late + 2 * KB + KD * SLOTS * 4)
        gate_a = at("gate_a", [P, 2, D], F32, late)
        gate_f = at("gate_f", [SLOTS, D], F32, late + 8 * KB)

        x_all = at("x_all", [P, TILES, D], F32, ST)
        zaT = at("zaT", [2 * RANK + 1, NTOK], F32, ST + 20 * KB)
        vecs = at("vecs", [V_ROWS, P], F32, ST + 23 * KB)
        lt = at("lt", [P, 2, 512], F32, ST)
        S = at("S", [P, 24, HP, DV], F32, ST)
        x2 = at("x2", [P, TILES, D], F32, ST)

        xn = at("xn", [P, TILES, D], F32, DR)
        pos_sb = at("pos_sb", [P, T_LAT, D], F32, DR + 20 * KB)
        junk = at("junk", [P, D], F32, DR + 36 * KB)
        htmp = at("htmp", [P, 2, NTOK], F32, DR + 20 * KB)
        proj = at("proj", [P, TILES, 4, 512], F32, DR)
        mix = at("mix", [P, TILES, 2, KD, P], F32R, DR)

        hT_hi = at("hT_hi", [P, KD, NTOK], F32R, HT)
        hT_lo = at("hT_lo", [P, KD, NTOK], F32R, HT + 20 * KB)
        qdec = at("qdec", [P, TILES, 4, P], F32, HT)
        attn = at("attn", [P, TILES, HEADS, P], F32, HT + 10 * KB)
        eb = at("eb", [P, 2, 4, P], F32, HT + 20 * KB)
        enb = at("enb", [P, 2, 4, P], F32, HT + 24 * KB)
        kint = at("kint", [P, 2, 4, P], F32, HT + 28 * KB)
        kstT = at("kstT", [P, 2, 4, P], F32, HT + 32 * KB)
        kst = at("kst", [P, 2, 4, P], F32, HT + 36 * KB)
        on = at("on", [P, TILES, HEADS, P], F32, HT + 20 * KB)
        pT = at("pT", [P, 4, NTOK], F32, HT + 30 * KB)
        ojunk = at("ojunk", [P, P], F32, DR)
        wtmp = at("wtmp", [P, 512], F32, EX + K_POOL * 4)
        junk2 = at("junk2", [P, D], F32, EX + K_COLS * 4)

        xn2 = at("xn2", [P, TILES, D], F32, DR)
        h2 = at("h2", [P, 2, NTOK], F32, DR + 20 * KB)
        lgT = at("lgT", [EXPERTS, NTOK], F32, DR + 25 * KB)
        xg = at("xg", [SLOTS, D], F32, DR + 28 * KB)
        xem = at("xem", [P, KD, SLOTS], F32, DR + 32 * KB)
        xe_hi = at("xe_hi", [P, KD, SLOTS], F32R, DR + 32 * KB + 2560)
        xe_lo = at("xe_lo", [P, KD, SLOTS], F32R, DR + 32 * KB + 5120)
        sg = at("sg", [SLOTS, 2, GROUP], F32, DR)
        hid = at("hid", [SLOTS, 2, GROUP], F32, DR + 2 * KB)
        hT2_hi = at("hT2_hi", [P, 2, 2, SLOTS], F32R, DR + 4 * KB)
        hT2_lo = at("hT2_lo", [P, 2, 2, SLOTS], F32R, DR + 4 * KB + 1280)
        yrow = at("yrow", [SLOTS, D], F32, DR + 8 * KB)
        tk = EX + K_COLS * 4 + 4 * KB
        prT = at("prT", [EXPERTS, NTOK], F32, DR + 25 * KB)
        pr = at("pr", [P, TILES, EXPERTS], F32, tk)
        prm = at("prm", [P, TILES], F32, tk + 320)
        prs = at("prs", [P, TILES], F32, tk + 352)
        gv = at("gv", [EXPERTS, SLOTS], F32, tk + 384)
        gi = at("gi", [EXPERTS, SLOTS], U32, tk + 704)
        gif = at("gif", [EXPERTS, SLOTS], F32, tk + 1024)
        gateT = at("gateT", [SLOTS, EXPERTS], F32, tk + 1344)
        idxT = at("idxT", [SLOTS, EXPERTS], U32, tk + 1408)
        idx_g = at("idx_g", [SLOTS, 1], U32, tk + 1472)
        idx_s = at("idx_s", [SLOTS, 1], U32, tk + 1504)
        gate_cur = at("gate_cur", [SLOTS, 1], F32, tk + 1536)
        acc_sb = at("acc_sb", [P, TILES, D], F32, HT)
        fin_g = at("fin_g", [P, D], F32, HT + 20 * KB)
        fjunk = at("fjunk", [P, D], F32, HT + 24 * KB)

        ident = const[:, K_ID:K_ID + P]
        tri = (const[:, K_TRIF:K_TRIF + P], const[:, K_TRIB:K_TRIB + P])

        def pool_mat(g, s):
            k = K_POOL + (2 * g + s) * P
            return const[:, k:k + P]

        def sel(n, width):
            return const[0:5, K_SEL + n * P:K_SEL + n * P + width]

        bank = [ctx.enter_context(nc.psum_tensor(f"bank{n}", [P, 512], F32)) for n in range(8)]

        def o_bank(t, par):
            b = bank[(0, 1, 2)[t // 2] if par == 0 else (3, 4, 7)[t // 2]]
            return b[:, t % 2 * 256:t % 2 * 256 + 256].rearrange("p (h v) -> p h v", h=HP)

        xs_dram = nc.dram_tensor("xs_dram", (NTOK, D), F32).ap()
        xn2_dram = nc.dram_tensor("xn2_dram", (NTOK, D), F32).ap()
        acc_dram = nc.dram_tensor("acc_dram", (NTOK, D), F32).ap()

        def sem(name):
            return ctx.enter_context(nc.semaphore(name))

        vec_in, const_in, xlat_in, xctx_in, pos_in = map(sem, ("vec_in", "const_in", "xlat_in", "xctx_in", "pos_in"))
        small_in, up_in, state_in, xs_out, x_back, fin_in = map(sem, ("small_in", "up_in", "state_in", "xs_out", "x_back", "fin_in"))
        bias_in = [sem(f"bias_in{n}") for n in range(2)]
        raw_full = [sem(f"raw_full{n}") for n in range(RING)]
        acc_out, xn2_out, xg_in, scattered, fin_n, out_done = map(sem, (
            "acc_out", "xn2_out", "xg_in", "scattered", "fin_n", "out_done"))
        acc_back = [sem(f"acc_back{t}") for t in range(TILES)]
        hi_done, lo_done, unit_used = map(sem, ("hi_done", "lo_done", "unit_used"))
        act_step, dve_step, pool_step = map(sem, ("act_step", "dve_step", "pool_step"))
        cleared, pool_turn = sem("cleared"), sem("pool_turn")
        vecT_ps, vecT_sb, cond_hi, cond_lo = map(sem, ("vecT_ps", "vecT_sb", "cond_hi", "cond_lo"))
        x_pos, x_sq, x_rt, x_norm = map(sem, ("x_pos", "x_sq", "x_rt", "x_norm"))
        mod_row, mod_ps, mod_done = map(sem, ("mod_row", "mod_ps", "mod_done"))
        xT_ps, hl_done, hc_done, h_hi, h_lo = map(sem, ("xT_ps", "hl_done", "hc_done", "h_hi", "h_lo"))
        wza_h, wza_l, za_ps, za_sb = map(sem, ("wza_h", "wza_l", "za_ps", "za_sb"))
        la_ps, la_ln, la_done = map(sem, ("la_ps", "la_ln", "la_done"))
        win_ps, evac_act, evac_dve = map(sem, ("win_ps", "evac_act", "evac_dve"))
        g_s1, g_exp, g_kst, g_attn, g_kstT, g_mask, g_kcopy, g_kv, g_kvs = map(sem, (
            "g_s1", "g_exp", "g_kst", "g_attn", "g_kstT", "g_mask", "g_kcopy", "g_kv", "g_kvs"))
        scan_done, o_ps, o_sq, o_rt, o_n = map(sem, ("scan_done", "o_ps", "o_sq", "o_rt", "o_n"))
        p_ps, p_sb, m_ps, m_hi, m_lo = map(sem, ("p_ps", "p_sb", "m_ps", "m_hi", "m_lo"))
        wo_ps, wo_ev, x2_sq, x2_rt, x2_n = map(sem, ("wo_ps", "wo_ev", "x2_sq", "x2_rt", "x2_n"))
        r_ps, r_lat, r_ctx, r_lg, r_lgs, r_lt, r_sub, r_exp, r_pr, r_prT, r_prs = map(sem, (
            "r_ps", "r_lat", "r_ctx", "r_lg", "r_lgs", "r_lt", "r_sub", "r_exp", "r_pr", "r_prT", "r_prs"))
        topk, idx_ps, idx_sb = map(sem, ("topk", "idx_ps", "idx_sb"))
        xe_ps, xe_mul, xe_mod, xe_h, xe_l = map(sem, ("xe_ps", "xe_mul", "xe_mod", "xe_h", "xe_l"))
        silu_done, hid_done, hidT_ps, hidT_h, hidT_l, y_done, gate_set = map(sem, (
            "silu_done", "hid_done", "hidT_ps", "hidT_h", "hidT_l", "y_done", "gate_set"))
        y_free = sem("y_free")
        f_sq, f_rt, f_done = map(sem, ("f_sq", "f_rt", "f_done"))

        def rows(ap):
            return ap.rearrange("(k p) n -> p k n", p=P)

        def pre_source(n):
            kind, b, kh = PRE[n]
            if kind == "ada":
                w, c0 = w_ada[0], b * 512
            elif kind == "win":
                w, c0 = w_in[0], WIN_BLOCKS[b]
            else:
                w, c0 = w_out[0], b * 512
            return rows(w[kh * 512:(kh + 1) * 512, c0:c0 + 512])

        def expert_source(e, kind, g):
            cols = slice(g * GROUP, (g + 1) * GROUP)
            if kind == "down":
                return rows(w_e_down[0, e, cols, :])
            w = w_e_gate if kind == "gate" else w_e_up
            return rows(w[0, e, :, cols])

        def raw_need(j, i):
            before = NPRE // PRE_RING if j % RING < PRE_RING else 0
            return 16 * (before + j // RING + 1) + i * (16 * (EXP_UNITS // RING))

        def unit(j, i):
            return NPRE + j + i * EXP_UNITS

        def tile_rows(dram, s):
            lo, hi = (0, L_LAT) if s == LAT else (L_LAT, NTOK)
            return dram[lo:hi, :].rearrange("(t p) d -> p t d", p=P)

        block = ctx.enter_context(nc.Block())

        @block.sync
        def _(sp):
            def load(dst, src, done):
                sp.dma_start(dst, src).then_inc(done, 16)

            for row, v, n in ((V_C, c[0], KD), (V_CCTX, c_ctx, KD), (V_BADA, b_ada[0], 48),
                              (V_GMIX, norm_mix_g[0], KD), (V_GFFN, norm_ffn_g[0], KD),
                              (V_GGLA, gla_norm_g[0], 1), (V_PSC, pool_scale[0], 4)):
                load(vecs[row:row + n, :], v.rearrange("(k p) -> k p", p=P), vec_in)
            load(const[:, :], consts, const_in)
            load(x_all[:, 0:T_LAT, :], x_sample[0].rearrange("(t p) d -> p t d", p=P), xlat_in)
            load(x_all[:, T_LAT, :], x_prompt[0], xctx_in)
            load(pos_sb[:, :, :], pos.rearrange("(t p) d -> p t d", p=P), pos_in)
            for n in range(NPRE):
                if n >= PRE_RING:
                    sp.wait_ge(lo_done, n - PRE_RING + 1)
                load(raw[:, n % PRE_RING, :].rearrange("p (k n) -> p k n", k=4), pre_source(n),
                     raw_full[n % PRE_RING])
                if n == 2:
                    load(wza[:, :, :], rows(w_in[0, :, 1536:1568]), small_in)
                    load(wpool[:, :, :], w_pool[0].rearrange("g c d -> c g d"), small_in)
                    load(wrt[:, :, :], rows(w_router[0]), small_in)
                if n == WOUT0 - 1:
                    sp.wait_ge(o_ps, TILES)
                    sp.wait_ge(state_in, 16 * 8)
                    load(x2[:, 0:T_LAT, :], tile_rows(xs_dram, LAT), x_back)
                    load(x2[:, T_LAT, :], x_prompt[0], x_back)

            def expert_load(j, e):
                kind, g = UNITS[j]
                parts = 8 if kind != "down" else 2
                load(raw[:, j % RING, :].rearrange("p (k n) -> p k n", k=parts),
                     expert_source(e, kind, g), raw_full[j % RING])

            for j in range(EXP_UNITS):
                if j < PRE_RING:
                    sp.wait_ge(lo_done, NPRE - PRE_RING + j + 1)
                elif j == PRE_RING:
                    sp.wait_ge(m_lo, 16)
                elif j == 8:
                    sp.wait_ge(x2_n, TILES)
                    sp.wait_ge(acc_out, 32)
                elif j >= RING:
                    sp.wait_ge(lo_done, unit(j - RING, 0) + 1)
                expert_load(j, 0)
            with sp.Fori(1, EXPERTS) as i:
                for j in range(EXP_UNITS):
                    sp.wait_ge(lo_done, unit(j - RING, i) + 1)
                    expert_load(j, i)
            sp.wait_ge(lo_done, unit(0, EXPERTS))
            sp.dma_start(fin_g[:, :], final_norm_g.unsqueeze(0).broadcast_to([P, D])).then_inc(fin_in, 16)
            sp.wait_ge(scattered, 16 * EXPERTS)
            for t in range(TILES):
                load(acc_sb[:, t, :], acc_dram[t * P:(t + 1) * P, :], acc_back[t])
            for t in range(TILES):
                sp.wait_ge(f_done, t + 1)
                dst = y_sample[0, t * P:(t + 1) * P, :] if t < T_LAT else y_prompt[0]
                load(dst, acc_sb[:, t, :], out_done)
            sp.wait_ge(out_done, 16 * TILES)

        @block.gpsimd
        def _(pool):
            n = [0]

            def step(ins):
                n[0] += 1
                ins.then_inc(pool_step, 1)
                pool.wait_ge(pool_step, n[0])

            nc.gpsimd.memset(eps[:, :], EPS).then_inc(cleared, 1)
            nc.gpsimd.memset(cond[:, :, :].bitcast(F32), 0.0).then_inc(cleared, 1)
            nc.gpsimd.memset(wza_hi[:, :, :].bitcast(F32), 0.0).then_inc(cleared, 1)
            nc.gpsimd.memset(wza_lo[:, :, :].bitcast(F32), 0.0).then_inc(cleared, 1)
            pool.wait_ge(cleared, 4)
            nc.gpsimd.memset(zaT[2 * RANK:2 * RANK + 1, :], 1.0).then_inc(cleared, 1)
            pool.wait_ge(cleared, 5)
            step(nc.gpsimd.memset(wup[:, :], 0.0))
            hw = HEADS * DK
            pool.dma_start(wup[0:RANK, 0:hw], w_a_up_f[0]).then_inc(up_in, 16)
            pool.dma_start(wup[RANK:2 * RANK, hw:2 * hw], w_a_up_b[0]).then_inc(up_in, 16)
            pool.dma_start(wup[2 * RANK:2 * RANK + 1, 0:hw], b_a_f).then_inc(up_in, 16)
            pool.dma_start(wup[2 * RANK:2 * RANK + 1, hw:2 * hw], b_a_b).then_inc(up_in, 16)

            def bias_row(b):
                if b >= 2:
                    pool.wait_ge(mod_ps, b - 1)
                pool.dma_start(modrow[4:5, b % 2, :], b_ada[0:1, b * 512:(b + 1) * 512]).then_inc(bias_in[b % 2], 16)

            for b in range(ADA_FIRST):
                bias_row(b)
            pool.wait_ge(x_pos, 1)
            pool.dma_start(tile_rows(xs_dram, LAT), x_all[:, 0:T_LAT, :]).then_inc(xs_out, 16)
            pool.wait_ge(xs_out, 16)
            pool.wait_ge(la_done, TILES)
            for direction, st in ((0, state_fwd), (1, state_bwd)):
                t, ch = (0, 0) if direction == 0 else (T_LAT - 1, 1)
                slot = state_slot(t, ch, direction, True)
                for hp in range(HP):
                    pool.dma_start(S[:, slot, hp, :], st[0, 0, 2 * hp:2 * hp + 2].rearrange("a d v -> (a d) v")).then_inc(state_in, 16)
                slot = state_slot(T_LAT, 0 if direction == 0 else 1, direction, True)
                nc.gpsimd.memset(S[:, slot, :, :], 0.0).then_inc(cleared, 1)
            for b in range(ADA_FIRST, ADA_BLOCKS):
                bias_row(b)
                if b == ADA_FIRST + 1:
                    pool.wait_ge(scan_done, 1)
                    for direction, out in ((0, out_fwd), (1, out_bwd)):
                        slot = state_slot(T_LAT, 1 if direction == 0 else 0, direction, False)
                        for hp in range(HP):
                            pool.dma_start(out[0, 0, 2 * hp:2 * hp + 2].rearrange("a d v -> (a d) v"), S[:, slot, hp, :]).then_inc(state_in, 16)
            pool.wait_ge(wo_ev, 2 * TILES)
            pool.dma_start(tile_rows(acc_dram, LAT), x2[:, 0:T_LAT, :]).then_inc(acc_out, 16)
            pool.dma_start(acc_dram[L_LAT:NTOK, :], x2[:, T_LAT, :]).then_inc(acc_out, 16)
            pool.wait_ge(x2_n, TILES)
            pool.dma_start(tile_rows(xn2_dram, LAT), xn2[:, 0:T_LAT, :]).then_inc(xn2_out, 16)
            pool.dma_start(xn2_dram[L_LAT:NTOK, :], xn2[:, T_LAT, :]).then_inc(xn2_out, 16)
            pool.wait_ge(xn2_out, 32)

            def gather(e, k):
                step(nc.gpsimd.tensor_copy(idx_g[:, :], idxT[:, e]))
                nc.gpsimd.indirect_dma_start(
                    out=xg[:, :], out_offset=None, in_=xn2_dram[:, :],
                    in_offset=bass.IndirectOffsetOnAxis(ap=idx_g[:, 0:1], axis=0)).then_inc(xg_in, 16)

            pool.wait_ge(idx_sb, 2)
            gather(slice(0, 1), 0)
            steps0 = n[0]

            def rows_of(i, last):
                if not last:
                    pool.wait_ge(xe_ps, 2 * i + 2)
                    pool.wait_ge(xg_in, 16 * i + 16)
                    nc.gpsimd.tensor_copy(idx_g[:, :], idxT[:, bass.ds(i + 1, 1)]).then_inc(pool_step, 1)
                    pool.wait_ge(pool_step, 2 * i + steps0 + 1)
                    pool.sem_inc(pool_turn, 1)
                    nc.gpsimd.indirect_dma_start(
                        out=xg[:, :], out_offset=None, in_=xn2_dram[:, :],
                        in_offset=bass.IndirectOffsetOnAxis(ap=idx_g[:, 0:1], axis=0)).then_inc(xg_in, 16)
                nc.gpsimd.tensor_copy(idx_s[:, :], idxT[:, bass.ds(i, 1)]).then_inc(pool_step, 1)
                pool.wait_ge(pool_step, 2 * i + steps0 + (1 if last else 2))
                pool.wait_ge(y_done, 2 * i + 4)
                pool.sem_inc(pool_turn, 1)
                nc.gpsimd.indirect_dma_start(
                    out=acc_dram[:, :], out_offset=bass.IndirectOffsetOnAxis(ap=idx_s[:, 0:1], axis=0),
                    in_=yrow[:, :], in_offset=None,
                    compute_op=ALU.add).then_inc(scattered, 16)
                pool.wait_ge(scattered, 16 * i + 16)
                pool.sem_inc(y_free, 1)

            pool.wait_ge(acc_out, 32)
            pool.sem_inc(y_free, 1)
            with pool.Fori(0, EXPERTS - 1) as i:
                rows_of(i, False)
            rows_of(EXPERTS - 1, True)

        @block.scalar
        def _(act):
            n = [0]

            def step(ins):
                n[0] += 1
                ins.then_inc(act_step, 1)
                act.wait_ge(act_step, n[0])

            def high(u):
                act.wait_ge(raw_full[u % PRE_RING], 16 * (u // PRE_RING + 1))
                if u >= SPLIT:
                    act.wait_ge(unit_used, u - SPLIT + 1)
                nc.scalar.copy(w_hi[:, u % SPLIT, :], raw[:, u % PRE_RING, :]).then_inc(hi_done, 1)

            act.wait_ge(vecT_ps, 1)
            nc.scalar.copy(vecT[:, :], bank[7][:, 0:V_ROWS]).then_inc(vecT_sb, 1)
            act.wait_ge(vecT_sb, 1)
            step(nc.scalar.activation(silu_c[:, :], vecT[:, 0:16], ACT.Silu))
            act.wait_ge(cleared, 5)
            nc.scalar.copy(cond[:, :, 0:2], silu_c[:, :].rearrange("p (s k) -> p k s", s=2)).then_inc(cond_hi, 1)
            high(0)
            high(1)
            high(2)
            for t in range(TILES):
                if t == 0:
                    act.wait_ge(x_pos, 1)
                if t == T_LAT:
                    act.wait_ge(xctx_in, 16)
                nc.scalar.activation(junk[:, :], x_all[:, t, :], ACT.Square, accum_out=ss[:, t:t + 1]).then_inc(x_sq, 1)
                act.wait_ge(x_sq, t + 1)
            nc.scalar.activation(rstd[:, 0:TILES], ss[:, 0:TILES], ACT.Sqrt, bias=eps[:, :], scale=1.0 / D).then_inc(x_rt, 1)

            def mod_rows(b):
                act.wait_ge(unit_used, (2 * b + 2) if b < ADA_FIRST else ADA0 + 2 * (b - ADA_FIRST) + 2)
                if b >= 2:
                    act.wait_ge(mod_ps, b - 1)
                nc.scalar.copy(modrow[0:4, b % 2, :], bank[5 + b % 2][0:4, :]).then_inc(mod_row, 1)

            for b in range(ADA_FIRST):
                high(2 * b + 3)
                mod_rows(b)
                if b < ADA_FIRST - 1:
                    high(2 * b + 4)
            act.wait_ge(small_in, 48)
            nc.scalar.copy(wza_hi[:, :, 0:2 * RANK], wza[:, :, :]).then_inc(wza_h, 1)

            def h_lat(k):
                act.wait_ge(xT_ps, k + 1)
                if k == 0:
                    act.wait_ge(mod_done, ADA_FIRST + 1)
                if k >= 2:
                    act.wait_ge(h_lo, k - 1)
                nc.scalar.activation(htmp[:, k % 2, 0:L_LAT], bank[2 * (k % 2)][:, :], ACT.Identity,
                                     bias=modT[:, k, LAT:LAT + 1], scale=scaleA[:, k, LAT:LAT + 1]).then_inc(hl_done, 1)

            h_lat(0)
            for k in range(KD):
                if k + 1 < KD:
                    h_lat(k + 1)
                act.wait_ge(hl_done, k + 1)
                act.wait_ge(hc_done, k + 1)
                nc.scalar.copy(hT_hi[:, k, :], htmp[:, k % 2, :]).then_inc(h_hi, 1)
            high(WIN0 + 2)
            act.wait_ge(xs_out, 16)
            for t in range(TILES):
                act.wait_ge(la_ps, t + 1)
                if t >= 2:
                    act.wait_ge(la_done, t - 1)
                b = lt[:, t % 2, :]
                step(nc.scalar.activation(b, bank[5 + t % 2][:, :], ACT.Abs))
                step(nc.scalar.activation(b, b, ACT.Exp, scale=-1.0))
                nc.scalar.activation(b, b, ACT.Ln, bias=1.0).then_inc(la_ln, 1)
            for b in range(4):
                high(WIN0 + 2 * b + 3)
                for t in range(TILES) if b == 3 else range(0, TILES, 2):
                    if t < TILES - 1:
                        act.wait_ge(win_ps, (TILES - 1) * b + t + 1)
                    else:
                        act.wait_ge(unit_used, WIN0 + 2 * b + 2)
                    nc.scalar.activation(proj[:, t, b, :], bank[t][:, :], ACT.Silu if b == 3 else ACT.Copy).then_inc(evac_act, 1)
                high(WIN0 + 2 * b + 4)
            def gla_exp(t):
                act.wait_ge(g_s1, t + 1)
                if t >= 2:
                    act.wait_ge(g_mask, t - 1)
                bT = bank[t % 2][:, :].rearrange("p (c t) -> p c t", c=4)
                nc.scalar.activation(eb[:, t % 2], bT, ACT.Exp, scale=1.0 / 16).then_inc(g_exp, 1)
                nc.scalar.activation(enb[:, t % 2], bT, ACT.Exp, scale=-1.0 / 16).then_inc(g_exp, 1)

            gla_exp(0)
            for t in range(TILES):
                if t + 1 < TILES:
                    gla_exp(t + 1)
                act.wait_ge(g_kstT, t + 1)
                if t >= 2:
                    act.wait_ge(g_kv, 2 * (t - 1))
                nc.scalar.copy(kst[:, t % 2], bank[6][:, :].rearrange("p (c t) -> p c t", c=4)).then_inc(g_kcopy, 1)
                if t == 0:
                    act.wait_ge(xs_out, 16)
                    act.wait_ge(la_done, TILES)
                for ch in range(2):
                    act.wait_ge(g_kv, 2 * t + ch + 1)
                    kv = bank[7 - ch][:, :].rearrange("p (a h v) -> p a h v", a=2, h=HP)
                    for direction in range(2):
                        slot = state_slot(t, ch, direction, False)
                        nc.scalar.copy(S[:, slot], kv[:, direction]).then_inc(g_kvs, 1)
            for t in range(TILES):
                act.wait_ge(o_ps, min(t | 1, TILES - 1) + 1)
                for h in range(HEADS):
                    nc.scalar.activation(ojunk[:, :], o_bank(t, h % 2)[:, h // 2, :], ACT.Square,
                                         accum_out=ss[:, t * HEADS + h:t * HEADS + h + 1]).then_inc(o_sq, 1)
                    act.wait_ge(o_sq, t * HEADS + h + 1)
            nc.scalar.activation(rstd[:, :], ss[:, :], ACT.Sqrt, bias=eps[:, :], scale=1.0 / DV).then_inc(o_rt, 1)
            for b in range(ADA_FIRST, ADA_BLOCKS):
                u = ADA0 + 2 * (b - ADA_FIRST)
                high(u + 3)
                mod_rows(b)
                high(u + 4)
            for t in range(TILES):
                act.wait_ge(p_ps, t + 1)
                nc.scalar.copy(pT[:, :, t * P:(t + 1) * P], bank[t][:, :].rearrange("p (g t) -> p g t", g=4)).then_inc(p_sb, 1)
            for m in range(2 * HEADS):
                h = m % HEADS
                scale = vecT[:, V_GGLA:V_GGLA + 1] if m < HEADS else vecT[:, V_PSC + h:V_PSC + h + 1]
                act.wait_ge(m_ps, m + 1)
                nc.scalar.activation(mix[:, 0:T_LAT, 0, m, :], bank[5 + m % 2][:, :].rearrange("p (t n) -> p t n", t=T_LAT),
                                     ACT.Copy, scale=scale).then_inc(m_hi, 1)
                if h == HEADS - 1:
                    for q in range(HEADS):
                        col = vecT[:, V_GGLA:V_GGLA + 1] if m < HEADS else vecT[:, V_PSC + q:V_PSC + q + 1]
                        nc.scalar.activation(mix[:, T_LAT, 0, m - 3 + q, :], bank[7][:, q * P:(q + 1) * P], ACT.Copy, scale=col).then_inc(m_hi, 1)
            for u in range(WOUT0 + 3, NPRE):
                high(u)
            for t in range(TILES):
                act.wait_ge(wo_ev, TILES + t + 1)
                nc.scalar.activation(junk2[:, :], x2[:, t, :], ACT.Square, accum_out=ss[:, t:t + 1]).then_inc(x2_sq, 1)
                act.wait_ge(x2_sq, t + 1)
            nc.scalar.activation(rstd[:, 0:TILES], ss[:, 0:TILES], ACT.Sqrt, bias=eps[:, :], scale=1.0 / D).then_inc(x2_rt, 1)
            for k in range(KD):
                act.wait_ge(r_ps, k + 1)
                if k >= 2:
                    act.wait_ge(r_lg, k - 1)
                nc.scalar.activation(h2[:, k % 2, 0:L_LAT], bank[2 * (k % 2)][:, :], ACT.Identity,
                                     bias=modT[:, 24 + k, LAT:LAT + 1], scale=scaleF[:, k, LAT:LAT + 1]).then_inc(r_lat, 1)
            act.wait_ge(r_sub, 1)
            nc.scalar.activation(pr[:, :, :], pr[:, :, :], ACT.Exp).then_inc(r_exp, 1)

            def high_of(j, i):
                act.wait_ge(raw_full[j % RING], raw_need(j, i))
                act.wait_ge(unit_used, unit(j - SPLIT, i) + 1)
                nc.scalar.copy(w_hi[:, j % SPLIT, :], raw[:, j % RING, :]).then_inc(hi_done, 1)

            def rows_high(i):
                act.wait_ge(xe_mod, 2 * i + 2)
                nc.scalar.copy(xe_hi[:, :, :], xem[:, :, :]).then_inc(xe_h, 1)

            def silu(g, i):
                act.wait_ge(unit_used, unit(AT["up", g], i) + 1)
                nc.scalar.activation(sg[:, g % 2, :], bank[g % 2][0:SLOTS, 0:GROUP], ACT.Silu).then_inc(silu_done, 1)

            def hidden_high(g, i):
                act.wait_ge(hidT_ps, i * GROUPS + g + 1)
                nc.scalar.copy(hT2_hi[:, g % 2], bank[4 + g % 2][:, 0:2 * SLOTS].rearrange("p (c s) -> p c s", c=2)).then_inc(hidT_h, 1)

            def expert(i, last):
                high_of(2, i)
                high_of(3, i)
                high_of(4, i)
                silu(0, i)
                for g in range(1, GROUPS):
                    if g > 1:
                        high_of(3 * g + 1, i)
                    hidden_high(g - 1, i)
                    if 3 * g + 2 < EXP_UNITS:
                        high_of(3 * g + 2, i)
                    if 3 * g + 3 < EXP_UNITS:
                        high_of(3 * g + 3, i)
                    silu(g, i)
                if not last:
                    rows_high(i + 1)
                hidden_high(GROUPS - 1, i)
                if not last:
                    high_of(0, i + 1)
                    high_of(1, i + 1)

            act.wait_ge(xn2_out, 32)
            rows_high(0)
            high_of(0, 0)
            high_of(1, 0)
            with act.Fori(0, EXPERTS - 1) as i:
                expert(i, False)
            expert(EXPERTS - 1, True)
            act.wait_ge(fin_in, 16)
            for t in range(TILES):
                act.wait_ge(acc_back[t], 16)
                nc.scalar.activation(fjunk[:, :], acc_sb[:, t, :], ACT.Square, accum_out=ss[:, t:t + 1]).then_inc(f_sq, 1)
                act.wait_ge(f_sq, t + 1)
                nc.scalar.activation(rstd[:, t:t + 1], ss[:, t:t + 1], ACT.Sqrt, bias=eps[:, :], scale=1.0 / D).then_inc(f_rt, 1)

        @block.vector
        def _(dve):
            n = [0]

            def step(ins):
                n[0] += 1
                ins.then_inc(dve_step, 1)
                dve.wait_ge(dve_step, n[0])

            def low(u):
                dve.wait_ge(hi_done, u + 1)
                nc.vector.tensor_tensor(w_lo[:, u % SPLIT, :], raw[:, u % PRE_RING, :], w_hi[:, u % SPLIT, :], ALU.subtract).then_inc(lo_done, 1)

            dve.wait_ge(xlat_in, 16)
            dve.wait_ge(pos_in, 16)
            nc.vector.tensor_tensor(x_all[:, 0:T_LAT, :], x_all[:, 0:T_LAT, :], pos_sb[:, :, :], ALU.add).then_inc(x_pos, 1)
            dve.wait_ge(cond_hi, 1)
            nc.vector.tensor_tensor(cond[:, :, 2:4], silu_c[:, :].rearrange("p (s k) -> p k s", s=2), cond[:, :, 0:2], ALU.subtract).then_inc(cond_lo, 1)
            low(0)
            low(1)
            low(2)
            dve.wait_ge(x_rt, 1)
            step(nc.vector.reciprocal(rstd[:, 0:TILES], rstd[:, 0:TILES]))
            for t in range(TILES):
                nc.vector.tensor_scalar(xn[:, t, :], x_all[:, t, :], rstd[:, t:t + 1], None, ALU.mult).then_inc(x_norm, 1)

            def mod_columns(b):
                dve.wait_ge(mod_ps, b + 1)
                q = bank[7][:, 32 * (b % 2):32 * (b % 2) + 20].rearrange("p (j r) -> p j r", j=4)
                bias = vecT[:, V_BADA + 4 * b:V_BADA + 4 * b + 4].unsqueeze(2).broadcast_to([P, 4, 2])
                step(nc.vector.tensor_tensor(modP[:, :, :], q[:, :, 0:2], bias, ALU.add))
                nc.vector.tensor_tensor(modT[:, 4 * b:4 * b + 4, :], modP[:, :, :], q[:, :, 2:4], ALU.add).then_inc(mod_done, 1)

            for b in range(ADA_FIRST):
                low(2 * b + 3)
                mod_columns(b)
                if b < ADA_FIRST - 1:
                    low(2 * b + 4)
            dve.wait_ge(mod_done, ADA_FIRST)
            gm = vecT[:, V_GMIX:V_GMIX + KD].unsqueeze(2).broadcast_to([P, KD, 2])
            nc.vector.scalar_tensor_tensor(out=scaleA[:, :, :], in0=modT[:, 8:16, :], scalar=1.0, in1=gm, op0=ALU.add, op1=ALU.mult).then_inc(mod_done, 1)
            dve.wait_ge(mod_done, ADA_FIRST + 1)
            dve.wait_ge(wza_h, 1)
            nc.vector.tensor_tensor(wza_lo[:, :, 0:2 * RANK], wza[:, :, :], wza_hi[:, :, 0:2 * RANK], ALU.subtract).then_inc(wza_l, 1)

            def h_ctx(k):
                dve.wait_ge(xT_ps, k + 1)
                if k >= 2:
                    dve.wait_ge(h_lo, k - 1)
                nc.vector.tensor_scalar(htmp[:, k % 2, L_LAT:NTOK], bank[2 * (k % 2) + 1][:, 0:P], scaleA[:, k, CTX:CTX + 1],
                                        modT[:, k, CTX:CTX + 1], ALU.mult, ALU.add).then_inc(hc_done, 1)

            h_ctx(0)
            for k in range(KD):
                if k + 1 < KD:
                    h_ctx(k + 1)
                dve.wait_ge(h_hi, k + 1)
                nc.vector.tensor_tensor(hT_lo[:, k, :], htmp[:, k % 2, :], hT_hi[:, k, :], ALU.subtract).then_inc(h_lo, 1)
            low(WIN0 + 2)
            dve.wait_ge(za_ps, 1)
            nc.vector.tensor_copy(zaT[0:2 * RANK, 0:L_LAT], bank[5][0:2 * RANK, :]).then_inc(za_sb, 1)
            nc.vector.tensor_copy(zaT[0:2 * RANK, L_LAT:NTOK], bank[6][0:2 * RANK, 0:P]).then_inc(za_sb, 1)
            for t in range(TILES):
                dve.wait_ge(la_ln, t + 1)
                nc.vector.scalar_tensor_tensor(out=la[:, t, :], in0=bank[5 + t % 2][:, :], scalar=0.0, in1=lt[:, t % 2, :],
                                               op0=ALU.min, op1=ALU.subtract).then_inc(la_done, 1)
            for b in range(4):
                low(WIN0 + 2 * b + 3)
                for t in () if b == 3 else range(1, TILES, 2):
                    dve.wait_ge(win_ps, (TILES - 1) * b + t + 1)
                    nc.vector.tensor_copy(proj[:, t, b, :], bank[t][:, :]).then_inc(evac_dve, 1)
                low(WIN0 + 2 * b + 4)
            def gla_decays(t):
                s = t % 2
                qk = bank[2 + s][:, :].rearrange("p (a h t) -> p a h t", a=2, h=HP)
                dve.wait_ge(g_exp, 2 * t + 2)
                if t >= 2:
                    dve.wait_ge(g_kstT, t - 1)
                ebs = eb[:, s].rearrange("p (a h) t -> p a h t", a=2)
                ens = enb[:, s].rearrange("p (a h) t -> p a h t", a=2)
                kis = kint[:, s].rearrange("p (a h) t -> p a h t", a=2)
                kss = kstT[:, s].rearrange("p (a h) t -> p a h t", a=2)
                qds = qdec[:, t].rearrange("p (a h) t -> p a h t", a=2)
                for a in range(2):
                    end = ebs[:, a].rearrange("p h (c t) -> p h c t", c=2)[:, :, :, CHUNK - 1 if a == 0 else 0]
                    step(nc.vector.tensor_copy(dec[:, t, a], end))
                    step(nc.vector.scalar_tensor_tensor(out=qds[:, a], in0=qk[:, 0], scalar=DK ** -0.5, in1=ebs[:, a], op0=ALU.mult, op1=ALU.mult))
                    step(nc.vector.tensor_tensor(kis[:, a], qk[:, 1], ens[:, a], ALU.mult))
                for a in range(2):
                    ins = nc.vector.tensor_tensor(kss[:, a].rearrange("p h (c t) -> p (h c) t", c=2),
                                                  kis[:, a].rearrange("p h (c t) -> p (h c) t", c=2),
                                                  dec[:, t, a].rearrange("p h c -> p (h c)").unsqueeze(2).broadcast_to([P, 4, CHUNK]), ALU.mult)
                    if a == 0:
                        step(ins)
                    else:
                        ins.then_inc(g_kst, 1)
                        dve.wait_ge(g_kst, t + 1)

            gla_decays(0)
            for t in range(TILES):
                if t + 1 < TILES:
                    gla_decays(t + 1)
                dve.wait_ge(g_attn, t + 1)
                masks = const[:, K_TRIF:K_TRIF + 2 * P].rearrange("p (a t) -> p a t", a=2).unsqueeze(2).broadcast_to([P, 2, HP, P])
                for par in range(2):
                    scratch = (enb, kint)[par][:, t % 2].rearrange("p (a h) t -> p a h t", a=2)
                    step(nc.vector.tensor_tensor(scratch, bank[4 + par][:, :].rearrange("p (a h t) -> p a h t", a=2, h=HP), masks, ALU.mult))
                    ins = nc.vector.tensor_tensor(attn[:, t].rearrange("p (h q) t -> p h q t", q=2)[:, :, par], scratch[:, 0], scratch[:, 1], ALU.add)
                    if par == 0:
                        step(ins)
                    else:
                        ins.then_inc(g_mask, 1)
            dve.wait_ge(g_kvs, 4 * TILES)
            dve.wait_ge(state_in, 64)
            dve.wait_ge(cleared, 7)

            def scan(t, ch, direction, signal=None):
                a, b = state_slot(t, ch, direction, True), state_slot(t, ch, direction, False)
                for hp in range(HP):
                    ins = nc.vector.scalar_tensor_tensor(out=S[:, b, hp, :], in0=S[:, a, hp, :], scalar=dec[:, t, direction, hp, ch:ch + 1],
                                                         in1=S[:, b, hp, :], op0=ALU.mult, op1=ALU.add)
                    if signal is not None and hp == HP - 1:
                        ins.then_inc(signal, 1)
                    else:
                        step(ins)

            chunks = [(t, ch) for t in range(T_LAT) for ch in range(2)]
            for f, b in zip(chunks[:-1], reversed(chunks[1:])):
                scan(*f, 0)
                scan(*b, 1)
            scan(T_LAT, 0, 0)
            scan(T_LAT, 1, 1)
            scan(T_LAT, 1, 0)
            scan(T_LAT, 0, 1, scan_done)
            dve.wait_ge(o_rt, 1)
            step(nc.vector.reciprocal(rstd[:, :], rstd[:, :]))
            for t in range(TILES):
                dve.wait_ge(evac_act, 9 + t + 1)
                for par in range(2):
                    r = rstd[:, t * HEADS:(t + 1) * HEADS].rearrange("p (h q) -> p h q", q=2)[:, :, par].unsqueeze(2).broadcast_to([P, HP, DV])
                    step(nc.vector.tensor_tensor(on[:, t].rearrange("p (h q) v -> p h q v", q=2)[:, :, par], o_bank(t, par), r, ALU.mult))
                nc.vector.tensor_tensor(on[:, t], on[:, t], proj[:, t, 3, :].rearrange("p (h v) -> p h v", h=HEADS), ALU.mult).then_inc(o_n, 1)
            for b in range(ADA_FIRST, ADA_BLOCKS):
                u = ADA0 + 2 * (b - ADA_FIRST)
                low(u + 3)
                which, half = divmod(b, 2)
                if which == 2:
                    dve.wait_ge(mod_ps, b + 1)
                    step(nc.vector.tensor_copy(gate_a[:, LAT, half * 512:half * 512 + 512], bank[7][:, :]))
                    nc.vector.tensor_copy(gate_a[:, CTX, half * 512:half * 512 + 512], bank[0][:, :]).then_inc(mod_done, 1)
                elif which == 5:
                    dve.wait_ge(mod_ps, b + 1)
                    nc.vector.tensor_copy(gate_f[:, half * 512:half * 512 + 512], bank[7][0:SLOTS, :]).then_inc(mod_done, 1)
                else:
                    mod_columns(b)
                low(u + 4)
            dve.wait_ge(mod_done, ADA_BLOCKS + 1)
            gf = vecT[:, V_GFFN:V_GFFN + KD].unsqueeze(2).broadcast_to([P, KD, 2])
            nc.vector.scalar_tensor_tensor(out=scaleF[:, :, :], in0=modT[:, 32:40, :], scalar=1.0, in1=gf, op0=ALU.add, op1=ALU.mult).then_inc(mod_done, 1)
            for m in range(2 * HEADS):
                h = m % HEADS
                scale = vecT[:, V_GGLA:V_GGLA + 1] if m < HEADS else vecT[:, V_PSC + h:V_PSC + h + 1]
                dve.wait_ge(m_hi, m + 1 + (4 if m >= HEADS else 0))
                nc.vector.scalar_tensor_tensor(out=mix[:, 0:T_LAT, 1, m, :], in0=bank[5 + m % 2][:, :].rearrange("p (t n) -> p t n", t=T_LAT),
                                               scalar=scale, in1=mix[:, 0:T_LAT, 0, m, :], op0=ALU.mult, op1=ALU.subtract).then_inc(m_lo, 1)
                if h == HEADS - 1:
                    dve.wait_ge(m_hi, m + 1 + HEADS + (4 if m >= HEADS else 0))
                    for q in range(HEADS):
                        col = vecT[:, V_GGLA:V_GGLA + 1] if m < HEADS else vecT[:, V_PSC + q:V_PSC + q + 1]
                        nc.vector.scalar_tensor_tensor(out=mix[:, T_LAT, 1, m - 3 + q, :], in0=bank[7][:, q * P:(q + 1) * P],
                                                       scalar=col, in1=mix[:, T_LAT, 0, m - 3 + q, :], op0=ALU.mult, op1=ALU.subtract).then_inc(m_lo, 1)
            for u in range(WOUT0 + 3, NPRE):
                low(u)
            dve.wait_ge(x_back, 32)
            for half in range(2):
                cols = slice(half * 512, half * 512 + 512)
                for t in range(TILES):
                    if t < TILES - 1:
                        dve.wait_ge(wo_ps, half * (TILES - 1) + t + 1)
                    else:
                        dve.wait_ge(unit_used, WOUT0 + 2 * half + 2)
                    step(nc.vector.tensor_tensor(wtmp[:, :], bank[t][:, :], gate_a[:, CTX if t == T_LAT else LAT, cols], ALU.mult))
                    nc.vector.tensor_tensor(x2[:, t, cols], x2[:, t, cols], wtmp[:, :], ALU.add).then_inc(wo_ev, 1)
                    dve.wait_ge(wo_ev, half * TILES + t + 1)
            dve.wait_ge(x2_rt, 1)
            step(nc.vector.reciprocal(rstd[:, 0:TILES], rstd[:, 0:TILES]))
            for t in range(TILES):
                nc.vector.tensor_scalar(xn2[:, t, :], x2[:, t, :], rstd[:, t:t + 1], None, ALU.mult).then_inc(x2_n, 1)
            dve.wait_ge(mod_done, ADA_BLOCKS + 2)
            for k in range(KD):
                dve.wait_ge(r_ps, k + 1)
                if k >= 2:
                    dve.wait_ge(r_lg, k - 1)
                nc.vector.tensor_scalar(h2[:, k % 2, L_LAT:NTOK], bank[2 * (k % 2) + 1][:, 0:P], scaleF[:, k, CTX:CTX + 1],
                                        modT[:, 24 + k, CTX:CTX + 1], ALU.mult, ALU.add).then_inc(r_ctx, 1)
            dve.wait_ge(r_lg, KD)
            nc.vector.tensor_copy(lgT[:, 0:L_LAT], bank[5][0:EXPERTS, :]).then_inc(r_lgs, 1)
            nc.vector.tensor_copy(lgT[:, L_LAT:NTOK], bank[6][0:EXPERTS, 0:P]).then_inc(r_lgs, 1)
            dve.wait_ge(r_lt, 1)
            lg = bank[7][:, 0:TILES * EXPERTS].rearrange("p (t e) -> p t e", t=TILES)
            wide = [P, TILES, EXPERTS]
            step(nc.vector.reduce_max(prm[:, :], lg, AX_X))
            nc.vector.tensor_tensor(pr[:, :, :], lg, prm[:, :].unsqueeze(2).broadcast_to(wide), ALU.subtract).then_inc(r_sub, 1)
            dve.wait_ge(r_exp, 1)
            step(nc.vector.reduce_sum(prs[:, :], pr[:, :, :], AX_X))
            step(nc.vector.reciprocal(prs[:, :], prs[:, :]))
            nc.vector.tensor_tensor(pr[:, :, :], pr[:, :, :], prs[:, :].unsqueeze(2).broadcast_to(wide), ALU.mult).then_inc(r_pr, 1)
            dve.wait_ge(r_prT, 1)
            step(nc.vector.tensor_copy(prT[:, 0:L_LAT], bank[0][0:EXPERTS, :]))
            step(nc.vector.tensor_copy(prT[:, L_LAT:NTOK], bank[1][0:EXPERTS, 0:P]))
            for work, slots in ((prT[:, 0:L_LAT], range(0, CAP_LAT, 8)), (prT[:, L_LAT:NTOK], range(CAP_LAT, SLOTS, 8))):
                for s in slots:
                    step(nc.vector.max(gv[:, s:s + 8], work))
                    step(nc.vector.max_index(gi[:, s:s + 8], gv[:, s:s + 8], work))
                    if s != slots[-1]:
                        step(nc.vector.match_replace(work, gv[:, s:s + 8], work, -1.0))
            step(nc.vector.tensor_copy(gif[:, :], gi[:, :]))
            nc.vector.tensor_scalar(gif[:, CAP_LAT:SLOTS], gif[:, CAP_LAT:SLOTS], float(L_LAT), None, ALU.add).then_inc(topk, 1)
            dve.wait_ge(idx_ps, 1)
            nc.vector.tensor_copy(gateT[:, :], bank[2][0:SLOTS, 0:EXPERTS]).then_inc(idx_sb, 1)
            nc.vector.tensor_copy(idxT[:, :], bank[2][0:SLOTS, EXPERTS:2 * EXPERTS]).then_inc(idx_sb, 1)
            dve.wait_ge(idx_sb, 2)

            def low_of(j, i):
                dve.wait_ge(hi_done, unit(j, i) + 1)
                nc.vector.tensor_tensor(w_lo[:, j % SPLIT, :], raw[:, j % RING, :], w_hi[:, j % SPLIT, :], ALU.subtract).then_inc(lo_done, 1)

            def modulate(i):
                for q in range(2):
                    dve.wait_ge(xe_ps, 2 * i + q + 1)
                    ps = bank[6 + q][:, 0:4 * SLOTS].rearrange("p (k s) -> p k s", k=4)
                    for s, lo, hi in ((LAT, 0, CAP_LAT), (CTX, CAP_LAT, SLOTS)):
                        nc.vector.tensor_tensor(xem[:, 4 * q:4 * q + 4, lo:hi], ps[:, :, lo:hi],
                                                scaleF[:, 4 * q:4 * q + 4, s].unsqueeze(2).broadcast_to([P, 4, hi - lo]), ALU.mult).then_inc(xe_mul, 1)
                dve.wait_ge(xe_mul, 4 * i + 4)
                for s, lo, hi in ((LAT, 0, CAP_LAT), (CTX, CAP_LAT, SLOTS)):
                    nc.vector.tensor_tensor(xem[:, :, lo:hi], xem[:, :, lo:hi],
                                            modT[:, 24:32, s].unsqueeze(2).broadcast_to([P, KD, hi - lo]), ALU.add).then_inc(xe_mod, 1)

            def rows_low(i):
                dve.wait_ge(xe_h, i + 1)
                nc.vector.tensor_tensor(xe_lo[:, :, :], xem[:, :, :], xe_hi[:, :, :], ALU.subtract).then_inc(xe_l, 1)

            def hidden(g, i):
                dve.wait_ge(silu_done, i * GROUPS + g + 1)
                nc.vector.tensor_tensor(hid[:, g % 2, :], sg[:, g % 2, :], bank[g % 2][0:SLOTS, GROUP:2 * GROUP], ALU.mult).then_inc(hid_done, 1)

            def hidden_low(g, i):
                dve.wait_ge(hidT_h, i * GROUPS + g + 1)
                nc.vector.tensor_tensor(hT2_lo[:, g % 2], bank[4 + g % 2][:, 0:2 * SLOTS].rearrange("p (c s) -> p c s", c=2),
                                        hT2_hi[:, g % 2], ALU.subtract).then_inc(hidT_l, 1)

            def expert(i, last):
                nc.vector.tensor_copy(gate_cur[:, :], gateT[:, bass.ds(i, 1)]).then_inc(gate_set, 1)
                low_of(2, i)
                low_of(3, i)
                low_of(4, i)
                hidden(0, i)
                for g in range(1, GROUPS):
                    if g > 1:
                        low_of(3 * g + 1, i)
                    hidden_low(g - 1, i)
                    if 3 * g + 2 < EXP_UNITS:
                        low_of(3 * g + 2, i)
                    if 3 * g + 3 < EXP_UNITS:
                        low_of(3 * g + 3, i)
                    hidden(g, i)
                    if g == 7 and not last:
                        modulate(i + 1)
                if not last:
                    rows_low(i + 1)
                hidden_low(GROUPS - 1, i)
                if not last:
                    low_of(0, i + 1)
                    low_of(1, i + 1)
                dve.wait_ge(unit_used, unit(0, i + 1))
                dve.wait_ge(gate_set, i + 1)
                dve.wait_ge(y_free, i + 1)
                for half in range(2):
                    cols = slice(half * 512, half * 512 + 512)
                    nc.vector.scalar_tensor_tensor(out=yrow[:, cols], in0=bank[2 + half][0:SLOTS, :], scalar=gate_cur[:, :],
                                                   in1=gate_f[:, cols], op0=ALU.mult, op1=ALU.mult).then_inc(y_done, 1)
                dve.wait_ge(y_done, 2 * i + 4)

            dve.sem_inc(y_done, 2)
            modulate(0)
            rows_low(0)
            low_of(0, 0)
            low_of(1, 0)
            dve.wait_ge(xn2_out, 32)
            with dve.Fori(0, EXPERTS - 1) as i:
                expert(i, False)
            expert(EXPERTS - 1, True)
            dve.wait_ge(fin_in, 16)
            for t in range(TILES):
                dve.wait_ge(f_rt, t + 1)
                step(nc.vector.reciprocal(rstd[:, t:t + 1], rstd[:, t:t + 1]))
                nc.vector.scalar_tensor_tensor(out=acc_sb[:, t, :], in0=acc_sb[:, t, :], scalar=rstd[:, t:t + 1], in1=fin_g[:, :],
                                               op0=ALU.mult, op1=ALU.mult).then_inc(f_done, 1)

        @block.tensor
        def _(pe):
            def product(out, xh, xl, wh, wl, first, last):
                nc.tensor.matmul(out, xh, wh, start=first, stop=False)
                nc.tensor.matmul(out, xh, wl, start=False, stop=False)
                return nc.tensor.matmul(out, xl, wh, start=False, stop=last)

            def split_ready(u):
                pe.wait_ge(hi_done, u + 1)
                pe.wait_ge(lo_done, u + 1)

            def parts(u, k):
                a = (u % SPLIT)
                return [w[:, a, :].rearrange("p (k n) -> p k n", k=k) for w in (w_hi, w_lo)]

            pe.wait_ge(vec_in, 16 * 7)
            pe.wait_ge(const_in, 16)
            nc.tensor.transpose(bank[7][:, 0:V_ROWS], vecs[:, :], ident[0:V_ROWS, 0:V_ROWS]).then_inc(vecT_ps, 1)
            pe.wait_ge(cond_hi, 1)
            pe.wait_ge(cond_lo, 1)

            def ada(b, u0):
                out = bank[5 + b % 2][:, :]
                if b >= 2:
                    pe.wait_ge(mod_row, b - 1)
                for kh in range(2):
                    split_ready(u0 + kh)
                    wh, wl = parts(u0 + kh, 4)
                    for k in range(4):
                        x = cond[:, 4 * kh + k, :]
                        nc.tensor.matmul(out, x, wh[:, k, :], start=kh + k == 0, stop=False)
                        last = nc.tensor.matmul(out, x, wl[:, k, :], start=False, stop=kh + k == 4)
                    last.then_inc(unit_used, 1)

            def ada_turn(b):
                pe.wait_ge(mod_row, b + 1)
                pe.wait_ge(bias_in[b % 2], 16 * (b // 2 + 1))
                row = modrow[:, b % 2, :]
                which = b // 2
                if b >= 1:
                    pe.wait_ge(mod_done, b + (b >= ADA_FIRST))
                if which in (2, 5):
                    if which == 2:
                        nc.tensor.matmul(bank[7][:, :], sel(0, P), row, start=True, stop=True)
                        nc.tensor.matmul(bank[0][:, :], sel(1, P), row, start=True, stop=True).then_inc(mod_ps, 1)
                    else:
                        nc.tensor.matmul(bank[7][0:SLOTS, :], sel(2, SLOTS), row, start=True, stop=True).then_inc(mod_ps, 1)
                    return
                for j in range(4):
                    q = 32 * (b % 2) + 5 * j
                    last = nc.tensor.transpose(bank[7][:, q:q + 5], row[:, j * P:(j + 1) * P], ident[0:5, 0:5])
                last.then_inc(mod_ps, 1)

            for b in range(ADA_FIRST):
                ada(b, 2 * b)
                if b == 0:
                    pe.wait_ge(vecT_sb, 1)
                if b >= 1:
                    ada_turn(b - 1)
            ada_turn(ADA_FIRST - 1)
            pe.wait_ge(x_norm, TILES)
            for k in range(KD):
                if k >= 2:
                    pe.wait_ge(hl_done, k - 1)
                    pe.wait_ge(hc_done, k - 1)
                for t in range(TILES):
                    dst = bank[2 * (k % 2)][:, t * P:(t + 1) * P] if t < T_LAT else bank[2 * (k % 2) + 1][:, 0:P]
                    last = nc.tensor.transpose(dst, xn[:, t, k * P:(k + 1) * P], ident)
                last.then_inc(xT_ps, 1)
            pe.wait_ge(wza_h, 1)
            pe.wait_ge(wza_l, 1)
            pe.wait_ge(mod_done, ADA_FIRST)
            for k in range(KD):
                pe.wait_ge(h_hi, k + 1)
                pe.wait_ge(h_lo, k + 1)
                for cols, out in ((slice(0, L_LAT), bank[5][0:SLOTS, :]), (slice(L_LAT, NTOK), bank[6][0:SLOTS, 0:P])):
                    last = product(out, wza_hi[:, k, :], wza_lo[:, k, :], hT_hi[:, k, cols], hT_lo[:, k, cols], k == 0, k == KD - 1)
            last.then_inc(za_ps, 1)
            for b in range(4):
                for kh in range(2):
                    u = WIN0 + 2 * b + kh
                    split_ready(u)
                    wh, wl = parts(u, 4)
                    for t in range(TILES):
                        tok = slice(t * P, (t + 1) * P)
                        if kh == 0 and b == 0 and t < 4:
                            pe.wait_ge(hl_done, KD)
                            pe.wait_ge(hc_done, KD)
                        if kh == 0 and b > 0:
                            if t % 2 == 0:
                                pe.wait_ge(evac_act, 3 * (b - 1) + t // 2 + 1)
                            else:
                                pe.wait_ge(evac_dve, 2 * (b - 1) + t // 2 + 1)
                        for k in range(4):
                            kk = 4 * kh + k
                            last = product(bank[t][:, :], hT_hi[:, kk, tok], hT_lo[:, kk, tok], wh[:, k, :], wl[:, k, :], kk == 0, kk == KD - 1)
                        if t == TILES - 1:
                            last.then_inc(unit_used, 1)
                        elif kh == 1:
                            last.then_inc(win_ps, 1)
                        if b == 0 and kh == 0:
                            if t == 0:
                                pe.wait_ge(za_sb, 2)
                                pe.wait_ge(up_in, 64)
                                pe.wait_ge(cleared, 5)
                            if t >= 2:
                                pe.wait_ge(la_done, t - 1)
                            nc.tensor.matmul(bank[5 + t % 2][:, :], zaT[:, tok], wup[:, :], start=True, stop=True).then_inc(la_ps, 1)

            def gla_1(t):
                s = t % 2
                if t == 0:
                    pe.wait_ge(evac_act, 3 * 3 + TILES)
                    pe.wait_ge(evac_dve, 2 * 3)
                    pe.wait_ge(la_done, TILES)
                if t >= 2:
                    pe.wait_ge(g_exp, 2 * (t - 1))
                    pe.wait_ge(g_kst, t - 1)
                for cq in range(4):
                    nc.tensor.transpose(bank[2 + s][:, cq * P:(cq + 1) * P], proj[:, t, 0, cq * P:(cq + 1) * P], ident)
                for cc in range(4):
                    last = nc.tensor.matmul(bank[s][:, cc * P:(cc + 1) * P], la[:, t, cc * P:(cc + 1) * P], tri[cc // 2], start=True, stop=True)
                last.then_inc(g_s1, 1)

            def gla_2(t):
                s = t % 2
                pe.wait_ge(g_kst, t + 1)
                if t >= 1:
                    pe.wait_ge(g_mask, t)
                for a in range(2):
                    for h in range(HEADS):
                        hp, r = h // 2, slice(h % 2 * DK, h % 2 * DK + DK)
                        cq = 2 * a + hp
                        last = nc.tensor.matmul(bank[4 + h % 2][:, cq * P:(cq + 1) * P], kint[r, s, 2 * a + hp, :], qdec[r, t, 2 * a + hp, :], start=True, stop=True)
                last.then_inc(g_attn, 1)
                if t >= 1:
                    pe.wait_ge(g_kvs, 4 * t)
                for cc in range(4):
                    last = nc.tensor.transpose(bank[6][:, cc * P:(cc + 1) * P], kstT[:, s, cc, :], ident)
                last.then_inc(g_kstT, 1)

            def gla_3(t):
                s = t % 2
                pe.wait_ge(g_kcopy, t + 1)
                for ch in range(2):
                    rows_ = slice(ch * CHUNK, (ch + 1) * CHUNK)
                    for a in range(2):
                        for h in range(HEADS):
                            hp, par = divmod(h, 2)
                            last = nc.tensor.matmul(bank[7 - ch][par * DK:par * DK + DK, (2 * a + hp) * DV:(2 * a + hp + 1) * DV],
                                                    kst[rows_, s, 2 * a + hp, par * DK:par * DK + DK],
                                                    proj[rows_, t, 1, h * DV:(h + 1) * DV], start=True, stop=True)
                    last.then_inc(g_kv, 1)

            gla_1(0)
            for t in range(TILES):
                if t + 1 < TILES:
                    gla_1(t + 1)
                gla_2(t)
                gla_3(t)
            pe.wait_ge(scan_done, 1)
            pe.wait_ge(g_mask, TILES)
            for t in range(TILES):
                for h in range(HEADS):
                    hp, r = h // 2, slice(h % 2 * DK, h % 2 * DK + DK)
                    cols = slice(h * DV, (h + 1) * DV)
                    out = o_bank(t, h % 2)[:, hp, :]
                    nc.tensor.matmul(out, attn[:, t, h, :], proj[:, t, 1, cols], start=True, stop=False)
                    for ch in range(2):
                        tok = slice(ch * CHUNK, (ch + 1) * CHUNK)
                        for a in range(2):
                            last = nc.tensor.matmul(out[tok, :], qdec[r, t, 2 * a + hp, tok],
                                                    S[r, state_slot(t, ch, a, True), hp, :], start=False, stop=a == 1)
                last.then_inc(o_ps, 1)
            for b in range(ADA_FIRST, ADA_BLOCKS):
                ada(b, ADA0 + 2 * (b - ADA_FIRST))
                if b > ADA_FIRST:
                    if b - 1 == ADA_FIRST:
                        pe.wait_ge(o_n, TILES)
                        pe.wait_ge(g_kvs, 4 * TILES)
                    ada_turn(b - 1)
            ada_turn(ADA_BLOCKS - 1)
            pe.wait_ge(mod_done, 7)
            for t in range(TILES):
                for g in range(4):
                    last = nc.tensor.matmul(bank[t][:, g * P:(g + 1) * P], proj[:, t, 2, g * P:(g + 1) * P],
                                            pool_mat(g, CTX if t == T_LAT else LAT), start=True, stop=True)
                last.then_inc(p_ps, 1)
            pe.wait_ge(mod_done, ADA_BLOCKS + 1)
            pe.wait_ge(p_sb, TILES)
            for m in range(2 * HEADS):
                h = m % HEADS
                if m >= 2:
                    pe.wait_ge(m_lo, m - 1 + (4 if m > HEADS + 1 else 0))
                if m == HEADS:
                    pe.wait_ge(m_lo, 8)
                if m < HEADS:
                    for t in range(TILES):
                        dst = bank[5 + m % 2][:, t * P:(t + 1) * P] if t < T_LAT else bank[7][:, h * P:(h + 1) * P]
                        last = nc.tensor.transpose(dst, on[:, t, h, :], ident)
                else:
                    nc.tensor.matmul(bank[5 + m % 2][:, :], wpool[:, h, :], pT[:, h, 0:L_LAT], start=True, stop=True)
                    last = nc.tensor.matmul(bank[7][:, h * P:(h + 1) * P], wpool[:, h, :], pT[:, h, L_LAT:NTOK], start=True, stop=True)
                last.then_inc(m_ps, 1)
            pe.wait_ge(m_hi, 16)
            pe.wait_ge(m_lo, 16)
            for half in range(2):
                for kh in range(2):
                    u = WOUT0 + 2 * half + kh
                    split_ready(u)
                    wh, wl = parts(u, 4)
                    for t in range(TILES):
                        if half == 1 and kh == 0:
                            pe.wait_ge(wo_ev, t + 1)
                        for k in range(4):
                            kk = 4 * kh + k
                            last = product(bank[t][:, :], mix[:, t, 0, kk, :], mix[:, t, 1, kk, :], wh[:, k, :], wl[:, k, :], kk == 0, kk == KD - 1)
                        if t == TILES - 1:
                            last.then_inc(unit_used, 1)
                        elif kh == 1:
                            last.then_inc(wo_ps, 1)
            pe.wait_ge(x2_n, TILES)
            pe.wait_ge(wo_ev, 2 * TILES)
            for k in range(KD + 1):
                if k < KD:
                    if k >= 2:
                        pe.wait_ge(r_lat, k - 1)
                        pe.wait_ge(r_ctx, k - 1)
                    for t in range(TILES):
                        dst = bank[2 * (k % 2)][:, t * P:(t + 1) * P] if t < T_LAT else bank[2 * (k % 2) + 1][:, 0:P]
                        last = nc.tensor.transpose(dst, xn2[:, t, k * P:(k + 1) * P], ident)
                    last.then_inc(r_ps, 1)
                if k >= 1:
                    q = k - 1
                    pe.wait_ge(r_lat, q + 1)
                    pe.wait_ge(r_ctx, q + 1)
                    nc.tensor.matmul(bank[5][0:EXPERTS, :], wrt[:, q, :], h2[:, q % 2, 0:L_LAT], start=q == 0, stop=q == KD - 1)
                    nc.tensor.matmul(bank[6][0:EXPERTS, 0:P], wrt[:, q, :], h2[:, q % 2, L_LAT:NTOK], start=q == 0, stop=q == KD - 1).then_inc(r_lg, 1)
            pe.wait_ge(r_lgs, 2)
            for t in range(TILES):
                last = nc.tensor.transpose(bank[7][:, t * EXPERTS:(t + 1) * EXPERTS], lgT[:, t * P:(t + 1) * P], ident[0:EXPERTS, 0:EXPERTS])
            last.then_inc(r_lt, 1)
            pe.wait_ge(r_pr, 1)
            for t in range(TILES):
                dst = bank[0][0:EXPERTS, t * P:(t + 1) * P] if t < T_LAT else bank[1][0:EXPERTS, 0:P]
                last = nc.tensor.transpose(dst, pr[:, t, :], ident)
            last.then_inc(r_prT, 1)
            pe.wait_ge(topk, 1)
            nc.tensor.transpose(bank[2][0:SLOTS, 0:EXPERTS], gv[:, :], ident[0:EXPERTS, 0:EXPERTS])
            nc.tensor.transpose(bank[2][0:SLOTS, EXPERTS:2 * EXPERTS], gif[:, :], ident[0:EXPERTS, 0:EXPERTS]).then_inc(idx_ps, 1)

            def turn_rows(i):
                pe.wait_ge(xg_in, 16 * i + 16)
                for q in range(2):
                    for k in range(4):
                        last = nc.tensor.transpose(bank[6 + q][:, k * SLOTS:(k + 1) * SLOTS], xg[:, (4 * q + k) * P:(4 * q + k + 1) * P],
                                                   ident[0:SLOTS, 0:SLOTS])
                    last.then_inc(xe_ps, 1)

            def into(kind, g, i):
                j = AT[kind, g]
                pe.wait_ge(hi_done, unit(j, i) + 1)
                pe.wait_ge(lo_done, unit(j, i) + 1)
                wh, wl = parts(j, KD)
                out = bank[g % 2][0:SLOTS, 0:GROUP] if kind == "gate" else bank[g % 2][0:SLOTS, GROUP:2 * GROUP]
                for k in range(KD):
                    last = product(out, xe_hi[:, k, :], xe_lo[:, k, :], wh[:, k, :], wl[:, k, :], k == 0, k == KD - 1)
                last.then_inc(unit_used, 1)

            def turn_hidden(g, i):
                pe.wait_ge(hid_done, i * GROUPS + g + 1)
                for q in range(2):
                    last = nc.tensor.transpose(bank[4 + g % 2][:, q * SLOTS:(q + 1) * SLOTS], hid[:, g % 2, q * P:(q + 1) * P],
                                               ident[0:SLOTS, 0:SLOTS])
                last.then_inc(hidT_ps, 1)

            def down(g, i):
                j = AT["down", g]
                pe.wait_ge(hi_done, unit(j, i) + 1)
                pe.wait_ge(lo_done, unit(j, i) + 1)
                pe.wait_ge(hidT_l, i * GROUPS + g + 1)
                if g == 0:
                    pe.wait_ge(y_done, 2 * i + 2)
                wh, wl = parts(j, 2)
                for q in range(2):
                    for half in range(2):
                        cols = slice(half * 512, half * 512 + 512)
                        last = product(bank[2 + half][0:SLOTS, :], hT2_hi[:, g % 2, q, :], hT2_lo[:, g % 2, q, :], wh[:, q, cols], wl[:, q, cols],
                                       g == 0 and q == 0, g == GROUPS - 1 and q == 1)
                last.then_inc(unit_used, 1)

            def expert(i, last):
                pe.wait_ge(xe_l, i + 1)
                into("gate", 0, i)
                into("up", 0, i)
                for g in range(1, GROUPS):
                    into("gate", g, i)
                    turn_hidden(g - 1, i)
                    into("up", g, i)
                    down(g - 1, i)
                    if g == 6 and not last:
                        turn_rows(i + 1)
                turn_hidden(GROUPS - 1, i)
                down(GROUPS - 1, i)

            turn_rows(0)
            with pe.Fori(0, EXPERTS - 1) as i:
                expert(i, False)
            expert(EXPERTS - 1, True)


_INS = ["x_prompt", "x_sample", "state_gla_fwd", "state_gla_bwd", "c", "c_ctx", "norm_mix_g", "w_ada", "b_ada", "w_in",
        "w_a_up_f", "b_a_f", "w_a_up_b", "b_a_b", "gla_norm_g", "w_pool", "pool_scale", "w_out", "norm_ffn_g",
        "w_router", "w_e_gate", "w_e_up", "w_e_down", "final_norm_g"]
_OUTS = [(1, L_CTX, D), (1, L_LAT, D), (1, 1, HEADS, DK, DV), (1, 1, HEADS, DK, DV)]


def shape_constants():
    import numpy as np

    k = np.zeros((P, K_COLS), np.float32)
    i = np.arange(P)
    same = i[:, None] // CHUNK == i[None, :] // CHUNK
    k[:, K_ID:K_ID + P] = np.eye(P)
    k[:, K_TRIF:K_TRIF + P] = same & (i[:, None] <= i[None, :])
    k[:, K_TRIB:K_TRIB + P] = same & (i[:, None] >= i[None, :])
    for g, w in enumerate(POOLS):
        for s, seg in ((LAT, GRID_W), (CTX, L_CTX)):
            start = i // seg * seg
            lo = np.maximum(i - w // 2, start)
            hi = np.minimum(i - w // 2 + w - 1, start + seg - 1)
            m = ((i[:, None] >= lo) & (i[:, None] <= hi)).astype(np.float32) / (hi - lo + 1).astype(np.float32)
            k[:, K_POOL + (2 * g + s) * P:K_POOL + (2 * g + s + 1) * P] = m - np.eye(P, dtype=np.float32)
    k[[0, 2, 4], K_SEL:K_SEL + P] = 1
    k[[1, 3, 4], K_SEL + P:K_SEL + 2 * P] = 1
    k[[0, 2, 4], K_SEL + 2 * P:K_SEL + 2 * P + CAP_LAT] = 1
    k[1, K_SEL + 2 * P + CAP_LAT:K_SEL + 2 * P + SLOTS] = 1
    k[3, K_SEL + 2 * P + CAP_LAT:K_SEL + 2 * P + SLOTS] = 1
    k[4, K_SEL + 2 * P + CAP_LAT:K_SEL + 2 * P + SLOTS] = 1
    rows_n = L_LAT // GRID_W
    row = np.repeat(np.arange(rows_n), GRID_W).astype(np.float32)
    col = np.tile(np.arange(GRID_W), rows_n).astype(np.float32)
    quarter = D // 4
    omega = (1.0 / (10000.0 ** (np.arange(quarter, dtype=np.float32) / np.float32(quarter)))).astype(np.float32)
    er, ec = row[:, None] * omega[None, :], col[:, None] * omega[None, :]
    pos = np.concatenate([np.sin(er), np.cos(er), np.sin(ec), np.cos(ec)], axis=-1).astype(np.float32)
    return k, pos


def kernel(**inputs):
    import numpy as np
    import concourse.bacc as bacc
    from concourse.bass_utils import run_bass_kernel_spmd

    nc = bacc.Bacc("TRN2", target_bir_lowering=False, num_devices=1)
    k, pos = shape_constants()
    arrays, args = {}, []
    for name, a in [(name, np.ascontiguousarray(inputs[name])) for name in _INS] + [("consts", k), ("pos", pos)]:
        arrays[f"in_{name}"] = a
        args.append(nc.dram_tensor(f"in_{name}", a.shape, F32, kind="ExternalInput").ap())
    for i, shape in enumerate(_OUTS):
        args.append(nc.dram_tensor(f"out_{i}", shape, F32, kind="ExternalOutput").ap())
    build(nc, *args)
    r = run_bass_kernel_spmd(nc, [arrays], core_ids=[0])
    return tuple(r.results[0][f"out_{i}"] for i in range(len(_OUTS)))
```

```python
from contextlib import ExitStack

import concourse.bass as bass
from concourse import mybir

F32 = mybir.dt.float32
F32R = mybir.dt.float32r
U32 = mybir.dt.uint32
ALU = mybir.AluOpType
ACT = mybir.ActivationFunctionType
AX_X = mybir.AxisListType.X

P = 128
D = 1024
KD = D // P
L_LAT, L_CTX = 512, 128
T_LAT = L_LAT // P
TILES = T_LAT + 1
NTOK = L_LAT + L_CTX
LAT, CTX = 0, 1
HEADS, DK, DV, CHUNK = 4, 64, 128, 64
HP = HEADS // 2
RANK = 16
POOLS = (2, 4, 8, 16)
GRID_W = 64
EXPERTS = 16
FF = 2816
CAP_LAT, CAP_CTX = 2 * L_LAT // EXPERTS, 2 * L_CTX // EXPERTS
SLOTS = CAP_LAT + CAP_CTX
EPS = 1e-6

UNIT = 2048
RING = 11
PRE_RING = 3
SPLIT = 3
GROUP = 256
GROUPS = FF // GROUP
EXP_UNITS = 3 * GROUPS
assert EXP_UNITS % RING == 0 and EXP_UNITS % SPLIT == 0

ADA_FIRST = 4
ADA_BLOCKS = 6 * D // 512
PRE = [("ada", b, kh) for b in range(ADA_FIRST) for kh in range(2)]
WIN_BLOCKS = (0, 512, 1568, 1024)
WIN0 = len(PRE)
PRE += [("win", b, kh) for b in range(4) for kh in range(2)]
ADA0 = len(PRE)
PRE += [("ada", b, kh) for b in range(ADA_FIRST, ADA_BLOCKS) for kh in range(2)]
WOUT0 = len(PRE)
PRE += [("wout", b, kh) for b in range(2) for kh in range(2)]
NPRE = len(PRE)
assert NPRE % PRE_RING == 0 and NPRE % SPLIT == 0

V_C, V_CCTX, V_BADA, V_GMIX, V_GFFN, V_GGLA, V_PSC, V_ROWS = 0, 8, 16, 64, 72, 80, 81, 85
K_ID, K_TRIF, K_TRIB, K_POOL, K_COLS = 0, 128, 256, 384, 384 + 8 * 128


def expert_units():
    order = [("gate", 0), ("up", 0)]
    for g in range(1, GROUPS):
        order += [("gate", g), ("up", g), ("down", g - 1)]
    return order + [("down", GROUPS - 1)]


UNITS = expert_units()
AT = {u: j for j, u in enumerate(UNITS)}


def state_slot(t, c, direction, start):
    first = (0, 9)[direction] if t < T_LAT else (18, 21)[direction]
    n = (2 * t if t < T_LAT else 0) + c
    return first + (n + (direction == 1) if start else n + (direction == 0))


def build(nc, x_prompt, x_sample, state_fwd, state_bwd, c, c_ctx, norm_mix_g, w_ada, b_ada, w_in,
          w_a_up_f, b_a_f, w_a_up_b, b_a_b, gla_norm_g, w_pool, pool_scale, w_out, norm_ffn_g,
          w_router, w_e_gate, w_e_up, w_e_down, final_norm_g, consts, pos, y_prompt, y_sample,
          out_fwd, out_bwd):
    ctx = ExitStack()
    with ctx:
        base = (nc.sbuf_base + 63) // 64 * 64
        KB = 1024
        RAW = base
        HT = RAW + PRE_RING * UNIT * 4
        ST = HT + 40 * KB
        SPL = RAW + RING * UNIT * 4
        DR = SPL + 2 * SPLIT * UNIT * 4
        EX = DR + 40 * KB

        def at(name, shape, dt, offset):
            return nc.alloc_sbuf_tensor_at(name, shape, dt, offset=offset)

        raw = at("raw", [P, RING, UNIT], F32, RAW)
        w_hi = at("w_hi", [P, SPLIT, UNIT], F32R, SPL)
        w_lo = at("w_lo", [P, SPLIT, UNIT], F32R, SPL + SPLIT * UNIT * 4)

        here = [EX]

        def keep(name, shape, dt=F32):
            size = 4
            for n in shape[1:]:
                size *= n
            t = at(name, shape, dt, here[0])
            here[0] += (size + 31) // 32 * 32
            return t

        const = keep("const", [P, K_COLS])
        cond = keep("cond", [P, KD, P], F32R)
        wpool = keep("wpool", [P, 4, P])
        wrt = keep("wrt", [P, KD, EXPERTS])
        vecT = keep("vecT", [P, V_ROWS])
        silu_c = keep("silu_c", [P, 16])
        modT = keep("modT", [P, 48, 2])
        modP = keep("modP", [P, 4, 2])
        scaleA = keep("scaleA", [P, KD, 2])
        scaleF = keep("scaleF", [P, KD, 2])
        eps = keep("eps", [P, 1])
        ss = keep("ss", [P, 20])
        rstd = keep("rstd", [P, 20])
        dec = keep("dec", [P, TILES, 2, HP, 2])
        modrow = keep("modrow", [4, 2, 512])
        wza = keep("wza", [P, KD, 2 * RANK])
        late = here[0]
        wup = keep("wup", [2 * RANK + 1, 512])
        la = keep("la", [P, TILES, 512])
        assert here[0] <= nc.sbuf_usable_end, (here[0], nc.sbuf_usable_end)
        wza_hi = at("wza_hi", [P, KD, SLOTS], F32R, late + 2 * KB)
        wza_lo = at("wza_lo", [P, KD, SLOTS], F32R, late + 2 * KB + KD * SLOTS * 4)
        gate_a = at("gate_a", [P, 2, D], F32, late)
        gate_f = at("gate_f", [SLOTS, D], F32, late + 8 * KB)

        x_all = at("x_all", [P, TILES, D], F32, ST)
        zaT = at("zaT", [2 * RANK + 1, NTOK], F32, ST + 20 * KB)
        vecs = at("vecs", [V_ROWS, P], F32, ST + 23 * KB)
        lt = at("lt", [P, TILES, 512], F32, ST)
        S = at("S", [P, 24, HP, DV], F32, ST)
        x2 = at("x2", [P, TILES, D], F32, ST)

        xn = at("xn", [P, TILES, D], F32, DR)
        pos_sb = at("pos_sb", [P, T_LAT, D], F32, DR + 20 * KB)
        junk = at("junk", [P, D], F32, DR + 36 * KB)
        htmp = at("htmp", [P, 2, NTOK], F32, DR + 20 * KB)
        proj = at("proj", [P, TILES, 4, 512], F32, DR)
        mix = at("mix", [P, TILES, 2, KD, P], F32R, DR)

        hT_hi = at("hT_hi", [P, KD, NTOK], F32R, HT)
        hT_lo = at("hT_lo", [P, KD, NTOK], F32R, HT + 20 * KB)
        qdec = at("qdec", [P, TILES, 4, P], F32, HT)
        attn = at("attn", [P, TILES, HEADS, P], F32, HT + 10 * KB)
        eb = at("eb", [P, 2, 4, P], F32, HT + 20 * KB)
        enb = at("enb", [P, 2, 4, P], F32, HT + 24 * KB)
        kint = at("kint", [P, 2, 4, P], F32, HT + 28 * KB)
        kstT = at("kstT", [P, 2, 4, P], F32, HT + 32 * KB)
        kst = at("kst", [P, 2, 4, P], F32, HT + 36 * KB)
        on = at("on", [P, TILES, HEADS, P], F32, HT + 20 * KB)
        pT = at("pT", [P, 4, NTOK], F32, HT + 30 * KB)
        ojunk = at("ojunk", [P, P], F32, DR)
        wtmp = at("wtmp", [P, 512], F32, EX + K_POOL * 4)
        junk2 = at("junk2", [P, D], F32, EX + K_COLS * 4)

        xn2 = at("xn2", [P, TILES, D], F32, DR)
        h2 = at("h2", [P, 2, NTOK], F32, DR + 20 * KB)
        lgT = at("lgT", [EXPERTS, NTOK], F32, DR + 25 * KB)
        xg = at("xg", [SLOTS, D], F32, DR + 28 * KB)
        xem = at("xem", [P, KD, SLOTS], F32, DR + 32 * KB)
        xe_hi = at("xe_hi", [P, KD, SLOTS], F32R, DR + 32 * KB + 2560)
        xe_lo = at("xe_lo", [P, KD, SLOTS], F32R, DR + 32 * KB + 5120)
        sg = at("sg", [SLOTS, 2, GROUP], F32, DR)
        hid = at("hid", [SLOTS, 2, GROUP], F32, DR + 2 * KB)
        hT2_hi = at("hT2_hi", [P, 2, 2, SLOTS], F32R, DR + 4 * KB)
        hT2_lo = at("hT2_lo", [P, 2, 2, SLOTS], F32R, DR + 4 * KB + 1280)
        yrow = at("yrow", [SLOTS, D], F32, DR + 8 * KB)
        tk = EX + K_COLS * 4 + 4 * KB
        prT = at("prT", [EXPERTS, NTOK], F32, DR + 25 * KB)
        pr = at("pr", [P, TILES, EXPERTS], F32, tk)
        prm = at("prm", [P, TILES], F32, tk + 320)
        prs = at("prs", [P, TILES], F32, tk + 352)
        gv = at("gv", [EXPERTS, SLOTS], F32, tk + 384)
        gi = at("gi", [EXPERTS, SLOTS], U32, tk + 704)
        gif = at("gif", [EXPERTS, SLOTS], F32, tk + 1024)
        gateT = at("gateT", [SLOTS, EXPERTS], F32, tk + 1344)
        idxT = at("idxT", [SLOTS, EXPERTS], U32, tk + 1408)
        idx_g = at("idx_g", [SLOTS, 1], U32, tk + 1472)
        idx_s = at("idx_s", [SLOTS, 1], U32, tk + 1504)
        gate_cur = at("gate_cur", [SLOTS, 1], F32, tk + 1536)
        acc_sb = at("acc_sb", [P, TILES, D], F32, HT)
        fin_g = at("fin_g", [P, D], F32, HT + 20 * KB)
        fjunk = at("fjunk", [P, D], F32, HT + 24 * KB)

        ident = const[:, K_ID:K_ID + P]
        tri = (const[:, K_TRIF:K_TRIF + P], const[:, K_TRIB:K_TRIB + P])

        def pool_mat(g, s):
            k = K_POOL + (2 * g + s) * P
            return const[:, k:k + P]

        bank = [ctx.enter_context(nc.psum_tensor(f"bank{n}", [P, 512], F32)) for n in range(8)]

        def ada_unit(b):
            return 2 * b if b < ADA_FIRST else ADA0 + 2 * (b - ADA_FIRST)

        def ada_bank(b):
            if b < ADA_FIRST:
                return bank[5 + b % 2]
            return bank[1 + 2 * (b % 2)] if b < ADA_FIRST + TILES else bank[5 + b % 2]

        def turn_bank(b):
            return bank[7] if b < ADA_FIRST else ada_bank(b)

        def mix_bank(m):
            return bank[m % 4][:, :]

        def mix_ctx(m):
            h = m % HEADS
            return bank[7 if m < HEADS else 4][:, h * P:(h + 1) * P]

        def o_bank(t, par):
            b = bank[(0, 1, 2)[t // 2] if par == 0 else (3, 4, 7)[t // 2]]
            return b[:, t % 2 * 256:t % 2 * 256 + 256].rearrange("p (h v) -> p h v", h=HP)

        xs_dram = nc.dram_tensor("xs_dram", (NTOK, D), F32).ap()
        xn2_dram = nc.dram_tensor("xn2_dram", (NTOK, D), F32).ap()
        acc_dram = nc.dram_tensor("acc_dram", (NTOK, D), F32).ap()

        def sem(name):
            return ctx.enter_context(nc.semaphore(name))

        vec_in, const_in = map(sem, ("vec_in", "const_in"))
        x_in = [sem(f"x_in{t}") for t in range(TILES)]
        small_in, up_in, state_in, xs_out, x_back, fin_in = map(sem, ("small_in", "up_in", "state_in", "xs_out", "x_back", "fin_in"))
        raw_full = [sem(f"raw_full{n}") for n in range(RING)]
        acc_out, xn2_out, xg_in, scattered, fin_n, out_done = map(sem, (
            "acc_out", "xn2_out", "xg_in", "scattered", "fin_n", "out_done"))
        acc_back = [sem(f"acc_back{t}") for t in range(TILES)]
        hi_done, lo_done, unit_used = map(sem, ("hi_done", "lo_done", "unit_used"))
        act_step, dve_step, pool_step = map(sem, ("act_step", "dve_step", "pool_step"))
        cleared, pool_turn = sem("cleared"), sem("pool_turn")
        vecT_ps, vecT_sb, cond_hi, cond_lo = map(sem, ("vecT_ps", "vecT_sb", "cond_hi", "cond_lo"))
        x_pos, x_sq, x_rt, x_norm = map(sem, ("x_pos", "x_sq", "x_rt", "x_norm"))
        mod_row, mod_ps, mod_done, gate_ps, gate_sb, gatef_sb = map(sem, ("mod_row", "mod_ps", "mod_done", "gate_ps", "gate_sb", "gatef_sb"))
        xT_ps, hl_done, hc_done, h_hi, h_lo = map(sem, ("xT_ps", "hl_done", "hc_done", "h_hi", "h_lo"))
        wza_h, wza_l, za_ps, za_sb = map(sem, ("wza_h", "wza_l", "za_ps", "za_sb"))
        la_ps, la_abs, la_exp, la_min, la_ln, la_done = map(sem, ("la_ps", "la_abs", "la_exp", "la_min", "la_ln", "la_done"))
        win_ps, evac_act, evac_dve = map(sem, ("win_ps", "evac_act", "evac_dve"))
        g_s1, g_exp, g_kst, g_attn, g_kstT, g_mask, g_kcopy, g_kv, g_kvs = map(sem, (
            "g_s1", "g_exp", "g_kst", "g_attn", "g_kstT", "g_mask", "g_kcopy", "g_kv", "g_kvs"))
        scan_done, o_ps, o_sq, o_rt, o_n = map(sem, ("scan_done", "o_ps", "o_sq", "o_rt", "o_n"))
        p_ps, p_sb, m_ps, m_hi, m_lo = map(sem, ("p_ps", "p_sb", "m_ps", "m_hi", "m_lo"))
        wo_ps, wo_ev, x2_sq, x2_rt, x2_n = map(sem, ("wo_ps", "wo_ev", "x2_sq", "x2_rt", "x2_n"))
        r_ps, r_lat, r_ctx, r_lg, r_lgs, r_lt, r_sub, r_exp, r_pr, r_prT, r_prs = map(sem, (
            "r_ps", "r_lat", "r_ctx", "r_lg", "r_lgs", "r_lt", "r_sub", "r_exp", "r_pr", "r_prT", "r_prs"))
        topk, idx_ps, idx_sb = map(sem, ("topk", "idx_ps", "idx_sb"))
        xe_ps, xe_mul, xe_mod, xe_h, xe_l = map(sem, ("xe_ps", "xe_mul", "xe_mod", "xe_h", "xe_l"))
        silu_done, hid_done, hidT_ps, hidT_h, hidT_l, y_done, gate_set = map(sem, (
            "silu_done", "hid_done", "hidT_ps", "hidT_h", "hidT_l", "y_done", "gate_set"))
        y_free = sem("y_free")
        f_sq, f_rt, f_done = map(sem, ("f_sq", "f_rt", "f_done"))

        def rows(ap):
            return ap.rearrange("(k p) n -> p k n", p=P)

        def pre_source(n):
            kind, b, kh = PRE[n]
            if kind == "ada":
                w, c0 = w_ada[0], b * 512
            elif kind == "win":
                w, c0 = w_in[0], WIN_BLOCKS[b]
            else:
                w, c0 = w_out[0], b * 512
            return rows(w[kh * 512:(kh + 1) * 512, c0:c0 + 512])

        def expert_source(e, kind, g):
            cols = slice(g * GROUP, (g + 1) * GROUP)
            if kind == "down":
                return rows(w_e_down[0, e, cols, :])
            w = w_e_gate if kind == "gate" else w_e_up
            return rows(w[0, e, :, cols])

        def raw_need(j, i):
            before = NPRE // PRE_RING if j % RING < PRE_RING else 0
            return 16 * (before + j // RING + 1) + i * (16 * (EXP_UNITS // RING))

        def unit(j, i):
            return NPRE + j + i * EXP_UNITS

        def tile_rows(dram, s):
            lo, hi = (0, L_LAT) if s == LAT else (L_LAT, NTOK)
            return dram[lo:hi, :].rearrange("(t p) d -> p t d", p=P)

        block = ctx.enter_context(nc.Block())

        @block.sync
        def _(sp):
            def load(dst, src, done):
                sp.dma_start(dst, src).then_inc(done, 16)

            for row, v, n in ((V_C, c[0], KD), (V_CCTX, c_ctx, KD), (V_BADA, b_ada[0], 48),
                              (V_GMIX, norm_mix_g[0], KD), (V_GFFN, norm_ffn_g[0], KD),
                              (V_GGLA, gla_norm_g[0], 1), (V_PSC, pool_scale[0], 4)):
                load(vecs[row:row + n, :], v.rearrange("(k p) -> k p", p=P), vec_in)
            load(const[:, :], consts, const_in)
            for n in range(NPRE):
                if n >= PRE_RING:
                    sp.wait_ge(lo_done, n - PRE_RING + 1)
                load(raw[:, n % PRE_RING, :].rearrange("p (k n) -> p k n", k=4), pre_source(n),
                     raw_full[n % PRE_RING])
                if n == 2:
                    load(wza[:, :, :], rows(w_in[0, :, 1536:1568]), small_in)
                    load(wpool[:, :, :], w_pool[0].rearrange("g c d -> c g d"), small_in)
                    load(wrt[:, :, :], rows(w_router[0]), small_in)

            def expert_load(j, e):
                kind, g = UNITS[j]
                parts = 8 if kind != "down" else 2
                load(raw[:, j % RING, :].rearrange("p (k n) -> p k n", k=parts),
                     expert_source(e, kind, g), raw_full[j % RING])

            for j in range(EXP_UNITS):
                if j < PRE_RING:
                    sp.wait_ge(lo_done, NPRE - PRE_RING + j + 1)
                elif j == PRE_RING:
                    sp.wait_ge(m_lo, 16)
                elif j == 8:
                    sp.wait_ge(x2_n, TILES)
                    sp.wait_ge(acc_out, 32)
                elif j >= RING:
                    sp.wait_ge(lo_done, unit(j - RING, 0) + 1)
                expert_load(j, 0)
            with sp.Fori(1, EXPERTS) as i:
                for j in range(EXP_UNITS):
                    sp.wait_ge(lo_done, unit(j - RING, i) + 1)
                    expert_load(j, i)
            sp.wait_ge(lo_done, unit(0, EXPERTS))
            sp.dma_start(fin_g[:, :], final_norm_g.unsqueeze(0).broadcast_to([P, D])).then_inc(fin_in, 16)
            sp.wait_ge(scattered, 16 * EXPERTS)
            for t in range(TILES):
                load(acc_sb[:, t, :], acc_dram[t * P:(t + 1) * P, :], acc_back[t])
            for t in range(TILES):
                sp.wait_ge(f_done, t + 1)
                dst = y_sample[0, t * P:(t + 1) * P, :] if t < T_LAT else y_prompt[0]
                load(dst, acc_sb[:, t, :], out_done)
            sp.wait_ge(out_done, 16 * TILES)

        @block.gpsimd
        def _(pool):
            n = [0]

            def step(ins):
                n[0] += 1
                ins.then_inc(pool_step, 1)
                pool.wait_ge(pool_step, n[0])

            nc.gpsimd.memset(eps[:, :], EPS).then_inc(cleared, 1)
            nc.gpsimd.memset(cond[:, :, :].bitcast(F32), 0.0).then_inc(cleared, 1)
            nc.gpsimd.memset(wza_hi[:, :, :].bitcast(F32), 0.0).then_inc(cleared, 1)
            nc.gpsimd.memset(wza_lo[:, :, :].bitcast(F32), 0.0).then_inc(cleared, 1)
            pool.wait_ge(cleared, 4)
            nc.gpsimd.memset(zaT[2 * RANK:2 * RANK + 1, :], 1.0).then_inc(cleared, 1)
            pool.wait_ge(cleared, 5)
            step(nc.gpsimd.memset(wup[:, :], 0.0))
            hw = HEADS * DK
            pool.dma_start(wup[0:RANK, 0:hw], w_a_up_f[0]).then_inc(up_in, 16)
            pool.dma_start(wup[RANK:2 * RANK, hw:2 * hw], w_a_up_b[0]).then_inc(up_in, 16)
            pool.dma_start(wup[2 * RANK:2 * RANK + 1, 0:hw], b_a_f).then_inc(up_in, 16)
            pool.dma_start(wup[2 * RANK:2 * RANK + 1, hw:2 * hw], b_a_b).then_inc(up_in, 16)

            pool.wait_ge(x_pos, T_LAT)
            pool.wait_ge(mod_done, ADA_FIRST + 1)
            pool.dma_start(tile_rows(xs_dram, LAT), x_all[:, 0:T_LAT, :]).then_inc(xs_out, 16)
            pool.wait_ge(xs_out, 16)
            pool.wait_ge(la_done, TILES)
            for direction, st in ((0, state_fwd), (1, state_bwd)):
                t, ch = (0, 0) if direction == 0 else (T_LAT - 1, 1)
                slot = state_slot(t, ch, direction, True)
                for hp in range(HP):
                    pool.dma_start(S[:, slot, hp, :], st[0, 0, 2 * hp:2 * hp + 2].rearrange("a d v -> (a d) v")).then_inc(state_in, 16)
                slot = state_slot(T_LAT, 0 if direction == 0 else 1, direction, True)
                nc.gpsimd.memset(S[:, slot, :, :], 0.0).then_inc(cleared, 1)
            pool.wait_ge(scan_done, HP)
            for direction, out in ((0, out_fwd), (1, out_bwd)):
                slot = state_slot(T_LAT, 1 if direction == 0 else 0, direction, False)
                for hp in range(HP):
                    pool.dma_start(out[0, 0, 2 * hp:2 * hp + 2].rearrange("a d v -> (a d) v"), S[:, slot, hp, :]).then_inc(state_in, 16)
            pool.wait_ge(o_ps, TILES)
            pool.wait_ge(state_in, 16 * 8)
            pool.dma_start(x2[:, 0:T_LAT, :], tile_rows(xs_dram, LAT)).then_inc(x_back, 16)
            pool.dma_start(x2[:, T_LAT, :], x_prompt[0]).then_inc(x_back, 16)
            pool.wait_ge(wo_ev, 2 * TILES)
            pool.dma_start(tile_rows(acc_dram, LAT), x2[:, 0:T_LAT, :]).then_inc(acc_out, 16)
            pool.dma_start(acc_dram[L_LAT:NTOK, :], x2[:, T_LAT, :]).then_inc(acc_out, 16)
            pool.wait_ge(x2_n, TILES)
            pool.dma_start(tile_rows(xn2_dram, LAT), xn2[:, 0:T_LAT, :]).then_inc(xn2_out, 16)
            pool.dma_start(xn2_dram[L_LAT:NTOK, :], xn2[:, T_LAT, :]).then_inc(xn2_out, 16)
            pool.wait_ge(xn2_out, 32)

            def gather(e, k):
                step(nc.gpsimd.tensor_copy(idx_g[:, :], idxT[:, e]))
                nc.gpsimd.indirect_dma_start(
                    out=xg[:, :], out_offset=None, in_=xn2_dram[:, :],
                    in_offset=bass.IndirectOffsetOnAxis(ap=idx_g[:, 0:1], axis=0)).then_inc(xg_in, 16)

            pool.wait_ge(idx_sb, 2)
            gather(slice(0, 1), 0)
            steps0 = n[0]

            def rows_of(i, last):
                if not last:
                    pool.wait_ge(xe_ps, 2 * i + 2)
                    pool.wait_ge(xg_in, 16 * i + 16)
                    nc.gpsimd.tensor_copy(idx_g[:, :], idxT[:, bass.ds(i + 1, 1)]).then_inc(pool_step, 1)
                    pool.wait_ge(pool_step, 2 * i + steps0 + 1)
                    pool.sem_inc(pool_turn, 1)
                    nc.gpsimd.indirect_dma_start(
                        out=xg[:, :], out_offset=None, in_=xn2_dram[:, :],
                        in_offset=bass.IndirectOffsetOnAxis(ap=idx_g[:, 0:1], axis=0)).then_inc(xg_in, 16)
                nc.gpsimd.tensor_copy(idx_s[:, :], idxT[:, bass.ds(i, 1)]).then_inc(pool_step, 1)
                pool.wait_ge(pool_step, 2 * i + steps0 + (1 if last else 2))
                pool.wait_ge(y_done, 2 * i + 4)
                pool.sem_inc(pool_turn, 1)
                nc.gpsimd.indirect_dma_start(
                    out=acc_dram[:, :], out_offset=bass.IndirectOffsetOnAxis(ap=idx_s[:, 0:1], axis=0),
                    in_=yrow[:, :], in_offset=None,
                    compute_op=ALU.add).then_inc(scattered, 16)
                pool.wait_ge(scattered, 16 * i + 16)
                pool.sem_inc(y_free, 1)

            pool.wait_ge(acc_out, 32)
            pool.sem_inc(y_free, 1)
            with pool.Fori(0, EXPERTS - 1) as i:
                rows_of(i, False)
            rows_of(EXPERTS - 1, True)

        @block.scalar
        def _(act):
            n = [0]

            def tokens(t):
                rows_ = slice(t * P, (t + 1) * P)
                act.dma_start(x_all[:, t, :], x_sample[0, rows_, :] if t < T_LAT else x_prompt[0]).then_inc(x_in[t], 16)
                if t < T_LAT:
                    act.dma_start(pos_sb[:, t, :], pos[rows_, :]).then_inc(x_in[t], 16)

            def step(ins):
                n[0] += 1
                ins.then_inc(act_step, 1)
                act.wait_ge(act_step, n[0])

            def high(u):
                act.wait_ge(raw_full[u % PRE_RING], 16 * (u // PRE_RING + 1))
                if u >= SPLIT:
                    act.wait_ge(unit_used, u - SPLIT + 1)
                nc.scalar.copy(w_hi[:, u % SPLIT, :], raw[:, u % PRE_RING, :]).then_inc(hi_done, 1)

            act.wait_ge(vecT_ps, 1)
            nc.scalar.copy(vecT[:, :], bank[7][:, 0:V_ROWS]).then_inc(vecT_sb, 1)
            act.wait_ge(vecT_sb, 1)
            step(nc.scalar.activation(silu_c[:, :], vecT[:, 0:16], ACT.Silu))
            act.wait_ge(cleared, 5)
            nc.scalar.copy(cond[:, :, 0:2], silu_c[:, :].rearrange("p (s k) -> p k s", s=2)).then_inc(cond_hi, 1)

            def square(t):
                act.wait_ge(*((x_pos, t + 1) if t < T_LAT else (x_in[t], 16)))
                nc.scalar.activation(junk[:, :], x_all[:, t, :], ACT.Square, accum_out=ss[:, t:t + 1]).then_inc(x_sq, 1)
                act.wait_ge(x_sq, t + 1)

            for t in range(TILES):
                tokens(t)
                high(t)
                if t >= 2:
                    square(t - 2)

            def mod_rows(b):
                act.wait_ge(unit_used, ada_unit(b) + 2)
                if b >= 2:
                    act.wait_ge(mod_ps, b - 1)
                nc.scalar.copy(modrow[:, b % 2, :], ada_bank(b)[0:4, :]).then_inc(mod_row, 1)

            mod_rows(0)
            high(5)
            square(3)
            mod_rows(1)
            high(6)
            high(7)
            mod_rows(2)
            square(4)
            nc.scalar.activation(rstd[:, 0:TILES], ss[:, 0:TILES], ACT.Sqrt, bias=eps[:, :], scale=1.0 / D).then_inc(x_rt, 1)
            act.wait_ge(small_in, 48)
            nc.scalar.copy(wza_hi[:, :, 0:2 * RANK], wza[:, :, :]).then_inc(wza_h, 1)
            high(8)
            mod_rows(3)

            def h_lat(k):
                act.wait_ge(xT_ps, k + 1)
                if k == 0:
                    act.wait_ge(mod_done, ADA_FIRST + 1)
                if k >= 2:
                    act.wait_ge(h_lo, k - 1)
                nc.scalar.activation(htmp[:, k % 2, 0:L_LAT], bank[2 * (k % 2)][:, :], ACT.Identity,
                                     bias=modT[:, k, LAT:LAT + 1], scale=scaleA[:, k, LAT:LAT + 1]).then_inc(hl_done, 1)

            h_lat(0)
            for k in range(KD):
                act.wait_ge(hl_done, k + 1)
                act.wait_ge(hc_done, k + 1)
                nc.scalar.copy(hT_hi[:, k, :], htmp[:, k % 2, :]).then_inc(h_hi, 1)
                if k == 3:
                    high(9)
                if k + 1 < KD:
                    h_lat(k + 1)
            act.wait_ge(xs_out, 16)
            for t in range(TILES):
                act.wait_ge(la_ps, t + 1)
                nc.scalar.activation(lt[:, t, :], bank[5 + t % 2][:, :], ACT.Abs).then_inc(la_abs, 1)
                act.wait_ge(la_abs, t + 1)
                nc.scalar.activation(lt[:, t, :], lt[:, t, :], ACT.Exp, scale=-1.0).then_inc(la_exp, 1)
            for t in range(TILES):
                act.wait_ge(la_exp, t + 1)
                nc.scalar.activation(lt[:, t, :], lt[:, t, :], ACT.Ln, bias=1.0).then_inc(la_ln, 1)
            high(10)
            for b in range(4):
                high(WIN0 + 2 * b + 3)
                for t in range(TILES) if b == 3 else range(0, TILES, 2):
                    if t < TILES - 1:
                        act.wait_ge(win_ps, (TILES - 1) * b + t + 1)
                    else:
                        act.wait_ge(unit_used, WIN0 + 2 * b + 2)
                    nc.scalar.activation(proj[:, t, b, :], bank[t][:, :], ACT.Silu if b == 3 else ACT.Copy).then_inc(evac_act, 1)
                high(WIN0 + 2 * b + 4)
            def gla_exp(t):
                act.wait_ge(g_s1, t + 1)
                if t >= 2:
                    act.wait_ge(g_mask, t - 1)
                bT = bank[0][:, :].rearrange("p (c t) -> p c t", c=4)
                nc.scalar.activation(eb[:, t % 2], bT, ACT.Exp, scale=1.0 / 16).then_inc(g_exp, 1)
                nc.scalar.activation(enb[:, t % 2], bT, ACT.Exp, scale=-1.0 / 16).then_inc(g_exp, 1)

            gla_exp(0)
            for t in range(TILES):
                if t + 1 < TILES:
                    gla_exp(t + 1)
                act.wait_ge(g_kstT, t + 1)
                if t >= 2:
                    act.wait_ge(g_kv, 2 * (t - 1))
                nc.scalar.copy(kst[:, t % 2], bank[6][:, :].rearrange("p (c t) -> p c t", c=4)).then_inc(g_kcopy, 1)
                high(ADA0 + 3 + 2 * t)
                mod_rows(ADA_FIRST + t)
                if t == 0:
                    act.wait_ge(xs_out, 16)
                    act.wait_ge(la_done, TILES)
                for ch in range(2):
                    act.wait_ge(g_kv, 2 * t + ch + 1)
                    kv = bank[7 - ch][:, :].rearrange("p (a h v) -> p a h v", a=2, h=HP)
                    for direction in range(2):
                        slot = state_slot(t, ch, direction, False)
                        nc.scalar.copy(S[:, slot], kv[:, direction]).then_inc(g_kvs, 1)
                high(ADA0 + 4 + 2 * t)
            for t in range(TILES):
                act.wait_ge(p_ps, t + 1)
                nc.scalar.copy(pT[:, :, t * P:(t + 1) * P], bank[5 + t % 2][:, :].rearrange("p (g t) -> p g t", g=4)).then_inc(p_sb, 1)
            high(ADA0 + 13)
            mod_rows(9)
            high(ADA0 + 14)
            for t in range(TILES):
                act.wait_ge(o_ps, min(t | 1, TILES - 1) + 1)
                for h in range(HEADS):
                    nc.scalar.activation(ojunk[:, :], o_bank(t, h % 2)[:, h // 2, :], ACT.Square,
                                         accum_out=ss[:, t * HEADS + h:t * HEADS + h + 1]).then_inc(o_sq, 1)
                    act.wait_ge(o_sq, t * HEADS + h + 1)
            nc.scalar.activation(rstd[:, :], ss[:, :], ACT.Sqrt, bias=eps[:, :], scale=1.0 / DV).then_inc(o_rt, 1)
            for q in range(4):
                act.wait_ge(gate_ps, q + 1)
                nc.scalar.copy(gate_a[:, q // 2, q % 2 * 512:q % 2 * 512 + 512], bank[5 + q % 2][:, :]).then_inc(gate_sb, 1)
            high(ADA0 + 15)
            mod_rows(10)
            high(WOUT0)
            for m in range(2 * HEADS):
                if m == HEADS:
                    high(WOUT0 + 1)
                    mod_rows(11)
                h = m % HEADS
                scale = vecT[:, V_GGLA:V_GGLA + 1] if m < HEADS else vecT[:, V_PSC + h:V_PSC + h + 1]
                act.wait_ge(m_ps, m + 1)
                nc.scalar.activation(mix[:, 0:T_LAT, 0, m, :], mix_bank(m).rearrange("p (t n) -> p t n", t=T_LAT),
                                     ACT.Copy, scale=scale).then_inc(m_hi, 1)
                if h == HEADS - 1:
                    for q in range(HEADS):
                        col = vecT[:, V_GGLA:V_GGLA + 1] if m < HEADS else vecT[:, V_PSC + q:V_PSC + q + 1]
                        nc.scalar.activation(mix[:, T_LAT, 0, m - 3 + q, :], mix_ctx(m - 3 + q), ACT.Copy, scale=col).then_inc(m_hi, 1)
            high(WOUT0 + 2)
            high(WOUT0 + 3)
            for t in range(TILES):
                act.wait_ge(wo_ev, TILES + t + 1)
                nc.scalar.activation(junk2[:, :], x2[:, t, :], ACT.Square, accum_out=ss[:, t:t + 1]).then_inc(x2_sq, 1)
                act.wait_ge(x2_sq, t + 1)
                nc.scalar.activation(rstd[:, t:t + 1], ss[:, t:t + 1], ACT.Sqrt, bias=eps[:, :], scale=1.0 / D).then_inc(x2_rt, 1)
            for k in range(KD):
                act.wait_ge(r_ps, k + 1)
                if k >= 2:
                    act.wait_ge(r_lg, k - 1)
                nc.scalar.activation(h2[:, k % 2, 0:L_LAT], bank[2 * (k % 2)][:, :], ACT.Identity,
                                     bias=modT[:, 24 + k, LAT:LAT + 1], scale=scaleF[:, k, LAT:LAT + 1]).then_inc(r_lat, 1)
            act.wait_ge(r_sub, 1)
            nc.scalar.activation(pr[:, :, :], pr[:, :, :], ACT.Exp).then_inc(r_exp, 1)

            def high_of(j, i):
                act.wait_ge(raw_full[j % RING], raw_need(j, i))
                act.wait_ge(unit_used, unit(j - SPLIT, i) + 1)
                nc.scalar.copy(w_hi[:, j % SPLIT, :], raw[:, j % RING, :]).then_inc(hi_done, 1)

            def rows_high(i):
                act.wait_ge(xe_mod, 2 * i + 2)
                nc.scalar.copy(xe_hi[:, :, :], xem[:, :, :]).then_inc(xe_h, 1)

            def silu(g, i):
                act.wait_ge(unit_used, unit(AT["up", g], i) + 1)
                nc.scalar.activation(sg[:, g % 2, :], bank[g % 2][0:SLOTS, 0:GROUP], ACT.Silu).then_inc(silu_done, 1)

            def hidden_high(g, i):
                act.wait_ge(hidT_ps, i * GROUPS + g + 1)
                nc.scalar.copy(hT2_hi[:, g % 2], bank[4 + g % 2][:, 0:2 * SLOTS].rearrange("p (c s) -> p c s", c=2)).then_inc(hidT_h, 1)

            def expert(i, last):
                high_of(2, i)
                high_of(3, i)
                high_of(4, i)
                silu(0, i)
                for g in range(1, GROUPS):
                    if g > 1:
                        high_of(3 * g + 1, i)
                    hidden_high(g - 1, i)
                    if 3 * g + 2 < EXP_UNITS:
                        high_of(3 * g + 2, i)
                    if 3 * g + 3 < EXP_UNITS:
                        high_of(3 * g + 3, i)
                    silu(g, i)
                if not last:
                    rows_high(i + 1)
                hidden_high(GROUPS - 1, i)
                if not last:
                    high_of(0, i + 1)
                    high_of(1, i + 1)

            high_of(0, 0)
            high_of(1, 0)
            act.wait_ge(xn2_out, 32)
            rows_high(0)
            with act.Fori(0, EXPERTS - 1) as i:
                expert(i, False)
            expert(EXPERTS - 1, True)
            act.wait_ge(fin_in, 16)
            for t in range(TILES):
                act.wait_ge(acc_back[t], 16)
                nc.scalar.activation(fjunk[:, :], acc_sb[:, t, :], ACT.Square, accum_out=ss[:, t:t + 1]).then_inc(f_sq, 1)
                act.wait_ge(f_sq, t + 1)
                nc.scalar.activation(rstd[:, t:t + 1], ss[:, t:t + 1], ACT.Sqrt, bias=eps[:, :], scale=1.0 / D).then_inc(f_rt, 1)

        @block.vector
        def _(dve):
            n = [0]

            def step(ins):
                n[0] += 1
                ins.then_inc(dve_step, 1)
                dve.wait_ge(dve_step, n[0])

            def part(ins):
                n[0] += 1
                ins.then_inc(dve_step, 1)

            def fence():
                dve.wait_ge(dve_step, n[0])

            def low(u):
                dve.wait_ge(hi_done, u + 1)
                nc.vector.tensor_tensor(w_lo[:, u % SPLIT, :], raw[:, u % PRE_RING, :], w_hi[:, u % SPLIT, :], ALU.subtract).then_inc(lo_done, 1)

            for t in range(TILES):
                if t == 0:
                    dve.wait_ge(cond_hi, 1)
                    nc.vector.tensor_tensor(cond[:, :, 2:4], silu_c[:, :].rearrange("p (s k) -> p k s", s=2), cond[:, :, 0:2], ALU.subtract).then_inc(cond_lo, 1)
                low(t)
                if t >= 1:
                    dve.wait_ge(x_in[t - 1], 32)
                    nc.vector.tensor_tensor(x_all[:, t - 1, :], x_all[:, t - 1, :], pos_sb[:, t - 1, :], ALU.add).then_inc(x_pos, 1)

            def mod_columns(b):
                dve.wait_ge(mod_ps, b + 1)
                if b >= 1:
                    dve.wait_ge(mod_done, b + (b >= ADA_FIRST))
                q = turn_bank(b)[:, 0:16].rearrange("p (j r) -> p j r", j=4)
                bias = vecT[:, V_BADA + 4 * b:V_BADA + 4 * b + 4].unsqueeze(2).broadcast_to([P, 4, 2])
                step(nc.vector.tensor_tensor(modP[:, :, :], q[:, :, 0:2], bias, ALU.add))
                nc.vector.tensor_tensor(modT[:, 4 * b:4 * b + 4, :], modP[:, :, :], q[:, :, 2:4], ALU.add).then_inc(mod_done, 1)

            low(5)
            mod_columns(0)
            low(6)
            low(7)
            mod_columns(1)
            dve.wait_ge(x_rt, 1)
            step(nc.vector.reciprocal(rstd[:, 0:TILES], rstd[:, 0:TILES]))
            for t in range(TILES):
                nc.vector.tensor_scalar(xn[:, t, :], x_all[:, t, :], rstd[:, t:t + 1], None, ALU.mult).then_inc(x_norm, 1)
            mod_columns(2)
            mod_columns(3)
            dve.wait_ge(mod_done, ADA_FIRST)
            gm = vecT[:, V_GMIX:V_GMIX + KD].unsqueeze(2).broadcast_to([P, KD, 2])
            nc.vector.scalar_tensor_tensor(out=scaleA[:, :, :], in0=modT[:, 8:16, :], scalar=1.0, in1=gm, op0=ALU.add, op1=ALU.mult).then_inc(mod_done, 1)
            dve.wait_ge(mod_done, ADA_FIRST + 1)
            dve.wait_ge(wza_h, 1)
            nc.vector.tensor_tensor(wza_lo[:, :, 0:2 * RANK], wza[:, :, :], wza_hi[:, :, 0:2 * RANK], ALU.subtract).then_inc(wza_l, 1)

            def h_ctx(k):
                dve.wait_ge(xT_ps, k + 1)
                if k >= 2:
                    dve.wait_ge(h_lo, k - 1)
                nc.vector.tensor_scalar(htmp[:, k % 2, L_LAT:NTOK], bank[2 * (k % 2) + 1][:, 0:P], scaleA[:, k, CTX:CTX + 1],
                                        modT[:, k, CTX:CTX + 1], ALU.mult, ALU.add).then_inc(hc_done, 1)

            h_ctx(0)
            for k in range(KD):
                dve.wait_ge(h_hi, k + 1)
                nc.vector.tensor_tensor(hT_lo[:, k, :], htmp[:, k % 2, :], hT_hi[:, k, :], ALU.subtract).then_inc(h_lo, 1)
                if k + 1 < KD:
                    h_ctx(k + 1)
                if k in (1, 4):
                    low(8 + k // 4)
            dve.wait_ge(za_ps, 1)
            nc.vector.tensor_copy(zaT[0:2 * RANK, 0:L_LAT], bank[5][0:2 * RANK, :]).then_inc(za_sb, 1)
            nc.vector.tensor_copy(zaT[0:2 * RANK, L_LAT:NTOK], bank[6][0:2 * RANK, 0:P]).then_inc(za_sb, 1)
            for t in range(TILES):
                dve.wait_ge(la_abs, t + 1)
                nc.vector.tensor_scalar(la[:, t, :], bank[5 + t % 2][:, :], 0.0, None, ALU.min).then_inc(la_min, 1)
            for t in range(TILES):
                dve.wait_ge(la_ln, t + 1)
                dve.wait_ge(la_min, t + 1)
                nc.vector.tensor_tensor(la[:, t, :], la[:, t, :], lt[:, t, :], ALU.subtract).then_inc(la_done, 1)
            low(10)
            for b in range(4):
                low(WIN0 + 2 * b + 3)
                for t in () if b == 3 else range(1, TILES, 2):
                    dve.wait_ge(win_ps, (TILES - 1) * b + t + 1)
                    nc.vector.tensor_copy(proj[:, t, b, :], bank[t][:, :]).then_inc(evac_dve, 1)
                low(WIN0 + 2 * b + 4)
            def gla_decays(t):
                s = t % 2
                qk = bank[2][:, :].rearrange("p (a h t) -> p a h t", a=2, h=HP)
                dve.wait_ge(g_exp, 2 * t + 2)
                if t >= 2:
                    dve.wait_ge(g_kstT, t - 1)
                ebs = eb[:, s].rearrange("p (a h) t -> p a h t", a=2)
                ens = enb[:, s].rearrange("p (a h) t -> p a h t", a=2)
                kis = kint[:, s].rearrange("p (a h) t -> p a h t", a=2)
                kss = kstT[:, s].rearrange("p (a h) t -> p a h t", a=2)
                qds = qdec[:, t].rearrange("p (a h) t -> p a h t", a=2)
                for a in range(2):
                    end = ebs[:, a].rearrange("p h (c t) -> p h c t", c=2)[:, :, :, CHUNK - 1 if a == 0 else 0]
                    part(nc.vector.tensor_copy(dec[:, t, a], end))
                    part(nc.vector.scalar_tensor_tensor(out=qds[:, a], in0=qk[:, 0], scalar=DK ** -0.5, in1=ebs[:, a], op0=ALU.mult, op1=ALU.mult))
                    part(nc.vector.tensor_tensor(kis[:, a], qk[:, 1], ens[:, a], ALU.mult))
                fence()
                for a in range(2):
                    ins = nc.vector.tensor_tensor(kss[:, a].rearrange("p h (c t) -> p (h c) t", c=2),
                                                  kis[:, a].rearrange("p h (c t) -> p (h c) t", c=2),
                                                  dec[:, t, a].rearrange("p h c -> p (h c)").unsqueeze(2).broadcast_to([P, 4, CHUNK]), ALU.mult)
                    if a == 0:
                        part(ins)
                    else:
                        ins.then_inc(g_kst, 1)

            def scores(t):
                dve.wait_ge(g_attn, t + 1)
                masks = const[:, K_TRIF:K_TRIF + 2 * P].rearrange("p (a t) -> p a t", a=2).unsqueeze(2).broadcast_to([P, 2, HP, P])
                scratch = [b[:, t % 2].rearrange("p (a h) t -> p a h t", a=2) for b in (enb, kint)]
                for par in range(2):
                    part(nc.vector.tensor_tensor(scratch[par], bank[4 + par][:, :].rearrange("p (a h t) -> p a h t", a=2, h=HP), masks, ALU.mult))
                fence()
                for par in range(2):
                    ins = nc.vector.tensor_tensor(attn[:, t].rearrange("p (h q) t -> p h q t", q=2)[:, :, par], scratch[par][:, 0], scratch[par][:, 1], ALU.add)
                    if par == 0:
                        part(ins)
                    else:
                        ins.then_inc(g_mask, 1)
                dve.wait_ge(g_mask, t + 1)
                fence()

            def scan(t, ch, direction, signal=None):
                a, b = state_slot(t, ch, direction, True), state_slot(t, ch, direction, False)
                for hp in range(HP):
                    ins = nc.vector.scalar_tensor_tensor(out=S[:, b, hp, :], in0=S[:, a, hp, :], scalar=dec[:, t, direction, hp, ch:ch + 1],
                                                         in1=S[:, b, hp, :], op0=ALU.mult, op1=ALU.add)
                    if signal is None:
                        part(ins)
                    else:
                        ins.then_inc(signal, 1)

            gla_decays(0)
            for t in range(TILES):
                if t + 1 < TILES:
                    gla_decays(t + 1)
                if t >= 1:
                    mod_columns(ADA_FIRST + t - 1)
                low(ADA0 + 3 + 2 * t)
                scores(t)
                if t >= 1:
                    if t == 1:
                        dve.wait_ge(state_in, 64)
                        dve.wait_ge(cleared, 7)
                    dve.wait_ge(g_kvs, 4 * t)
                    for ch in range(2):
                        scan(t - 1, ch, 0)
                        fence()
                low(ADA0 + 4 + 2 * t)
            mod_columns(ADA_FIRST + TILES - 1)
            dve.wait_ge(g_kvs, 4 * TILES)
            chunks = [(t, ch) for t in range(T_LAT) for ch in range(2)]
            for b in reversed(chunks[2:]):
                scan(*b, 1)
                if b == (T_LAT - 1, 1):
                    scan(T_LAT, 0, 0)
                    scan(T_LAT, 1, 1)
                elif b == (T_LAT - 1, 0):
                    scan(T_LAT, 1, 0)
                    scan(T_LAT, 0, 1)
                fence()
            scan(*chunks[1], 1, scan_done)
            low(ADA0 + 13)
            low(ADA0 + 14)
            mod_columns(9)
            dve.wait_ge(o_rt, 1)
            step(nc.vector.reciprocal(rstd[:, :], rstd[:, :]))
            for t in range(TILES):
                dve.wait_ge(evac_act, 9 + t + 1)
                for par in range(2):
                    r = rstd[:, t * HEADS:(t + 1) * HEADS].rearrange("p (h q) -> p h q", q=2)[:, :, par].unsqueeze(2).broadcast_to([P, HP, DV])
                    step(nc.vector.tensor_tensor(on[:, t].rearrange("p (h q) v -> p h q v", q=2)[:, :, par], o_bank(t, par), r, ALU.mult))
                nc.vector.tensor_tensor(on[:, t], on[:, t], proj[:, t, 3, :].rearrange("p (h v) -> p h v", h=HEADS), ALU.mult).then_inc(o_n, 1)
            low(ADA0 + 15)
            for m in range(2 * HEADS):
                if m == HEADS:
                    low(WOUT0)
                    mod_columns(10)
                    mod_columns(11)
                h = m % HEADS
                scale = vecT[:, V_GGLA:V_GGLA + 1] if m < HEADS else vecT[:, V_PSC + h:V_PSC + h + 1]
                dve.wait_ge(m_hi, m + 1 + (4 if m >= HEADS else 0))
                nc.vector.scalar_tensor_tensor(out=mix[:, 0:T_LAT, 1, m, :], in0=mix_bank(m).rearrange("p (t n) -> p t n", t=T_LAT),
                                               scalar=scale, in1=mix[:, 0:T_LAT, 0, m, :], op0=ALU.mult, op1=ALU.subtract).then_inc(m_lo, 1)
                if h == HEADS - 1:
                    dve.wait_ge(m_hi, m + 1 + HEADS + (4 if m >= HEADS else 0))
                    for q in range(HEADS):
                        col = vecT[:, V_GGLA:V_GGLA + 1] if m < HEADS else vecT[:, V_PSC + q:V_PSC + q + 1]
                        nc.vector.scalar_tensor_tensor(out=mix[:, T_LAT, 1, m - 3 + q, :], in0=mix_ctx(m - 3 + q),
                                                       scalar=col, in1=mix[:, T_LAT, 0, m - 3 + q, :], op0=ALU.mult, op1=ALU.subtract).then_inc(m_lo, 1)
            low(WOUT0 + 1)
            dve.wait_ge(mod_done, ADA_BLOCKS + 1)
            gf = vecT[:, V_GFFN:V_GFFN + KD].unsqueeze(2).broadcast_to([P, KD, 2])
            nc.vector.scalar_tensor_tensor(out=scaleF[:, :, :], in0=modT[:, 32:40, :], scalar=1.0, in1=gf, op0=ALU.add, op1=ALU.mult).then_inc(mod_done, 1)
            for half in range(2):
                dve.wait_ge(gate_ps, 5 + half)
                nc.vector.tensor_copy(gate_f[:, half * 512:half * 512 + 512], bank[5 + half][0:SLOTS, :]).then_inc(gatef_sb, 1)
            low(WOUT0 + 2)
            low(WOUT0 + 3)
            dve.wait_ge(gatef_sb, 2)
            dve.wait_ge(gate_sb, 4)
            def norm2(t):
                dve.wait_ge(x2_rt, t + 1)
                step(nc.vector.reciprocal(rstd[:, t:t + 1], rstd[:, t:t + 1]))
                nc.vector.tensor_scalar(xn2[:, t, :], x2[:, t, :], rstd[:, t:t + 1], None, ALU.mult).then_inc(x2_n, 1)

            dve.wait_ge(x_back, 32)
            for half in range(2):
                cols = slice(half * 512, half * 512 + 512)
                for t in range(TILES):
                    if t < TILES - 1:
                        dve.wait_ge(wo_ps, half * (TILES - 1) + t + 1)
                    else:
                        dve.wait_ge(unit_used, WOUT0 + 2 * half + 2)
                    step(nc.vector.tensor_tensor(wtmp[:, :], bank[t][:, :], gate_a[:, CTX if t == T_LAT else LAT, cols], ALU.mult))
                    nc.vector.tensor_tensor(x2[:, t, cols], x2[:, t, cols], wtmp[:, :], ALU.add).then_inc(wo_ev, 1)
                    dve.wait_ge(wo_ev, half * TILES + t + 1)
                    if half == 1 and t >= 1:
                        norm2(t - 1)
            norm2(TILES - 1)
            dve.wait_ge(mod_done, ADA_BLOCKS + 2)
            for k in range(KD):
                dve.wait_ge(r_ps, k + 1)
                if k >= 2:
                    dve.wait_ge(r_lg, k - 1)
                nc.vector.tensor_scalar(h2[:, k % 2, L_LAT:NTOK], bank[2 * (k % 2) + 1][:, 0:P], scaleF[:, k, CTX:CTX + 1],
                                        modT[:, 24 + k, CTX:CTX + 1], ALU.mult, ALU.add).then_inc(r_ctx, 1)
            dve.wait_ge(r_lg, KD)
            nc.vector.tensor_copy(lgT[:, 0:L_LAT], bank[5][0:EXPERTS, :]).then_inc(r_lgs, 1)
            nc.vector.tensor_copy(lgT[:, L_LAT:NTOK], bank[6][0:EXPERTS, 0:P]).then_inc(r_lgs, 1)
            dve.wait_ge(r_lt, 1)
            lg = bank[7][:, 0:TILES * EXPERTS].rearrange("p (t e) -> p t e", t=TILES)
            wide = [P, TILES, EXPERTS]
            step(nc.vector.reduce_max(prm[:, :], lg, AX_X))
            nc.vector.tensor_tensor(pr[:, :, :], lg, prm[:, :].unsqueeze(2).broadcast_to(wide), ALU.subtract).then_inc(r_sub, 1)
            dve.wait_ge(r_exp, 1)
            step(nc.vector.reduce_sum(prs[:, :], pr[:, :, :], AX_X))
            step(nc.vector.reciprocal(prs[:, :], prs[:, :]))
            nc.vector.tensor_tensor(pr[:, :, :], pr[:, :, :], prs[:, :].unsqueeze(2).broadcast_to(wide), ALU.mult).then_inc(r_pr, 1)
            dve.wait_ge(r_prT, 1)
            step(nc.vector.tensor_copy(prT[:, 0:L_LAT], bank[0][0:EXPERTS, :]))
            step(nc.vector.tensor_copy(prT[:, L_LAT:NTOK], bank[1][0:EXPERTS, 0:P]))
            for work, slots in ((prT[:, 0:L_LAT], range(0, CAP_LAT, 8)), (prT[:, L_LAT:NTOK], range(CAP_LAT, SLOTS, 8))):
                for s in slots:
                    step(nc.vector.max(gv[:, s:s + 8], work))
                    step(nc.vector.max_index(gi[:, s:s + 8], gv[:, s:s + 8], work))
                    if s != slots[-1]:
                        step(nc.vector.match_replace(work, gv[:, s:s + 8], work, -1.0))
            step(nc.vector.tensor_copy(gif[:, :], gi[:, :]))
            nc.vector.tensor_scalar(gif[:, CAP_LAT:SLOTS], gif[:, CAP_LAT:SLOTS], float(L_LAT), None, ALU.add).then_inc(topk, 1)
            dve.wait_ge(idx_ps, 1)
            nc.vector.tensor_copy(gateT[:, :], bank[2][0:SLOTS, 0:EXPERTS]).then_inc(idx_sb, 1)
            nc.vector.tensor_copy(idxT[:, :], bank[2][0:SLOTS, EXPERTS:2 * EXPERTS]).then_inc(idx_sb, 1)
            dve.wait_ge(idx_sb, 2)

            def low_of(j, i):
                dve.wait_ge(hi_done, unit(j, i) + 1)
                nc.vector.tensor_tensor(w_lo[:, j % SPLIT, :], raw[:, j % RING, :], w_hi[:, j % SPLIT, :], ALU.subtract).then_inc(lo_done, 1)

            def modulate(i):
                for q in range(2):
                    dve.wait_ge(xe_ps, 2 * i + q + 1)
                    ps = bank[6 + q][:, 0:4 * SLOTS].rearrange("p (k s) -> p k s", k=4)
                    for s, lo, hi in ((LAT, 0, CAP_LAT), (CTX, CAP_LAT, SLOTS)):
                        nc.vector.tensor_tensor(xem[:, 4 * q:4 * q + 4, lo:hi], ps[:, :, lo:hi],
                                                scaleF[:, 4 * q:4 * q + 4, s].unsqueeze(2).broadcast_to([P, 4, hi - lo]), ALU.mult).then_inc(xe_mul, 1)
                dve.wait_ge(xe_mul, 4 * i + 4)
                for s, lo, hi in ((LAT, 0, CAP_LAT), (CTX, CAP_LAT, SLOTS)):
                    nc.vector.tensor_tensor(xem[:, :, lo:hi], xem[:, :, lo:hi],
                                            modT[:, 24:32, s].unsqueeze(2).broadcast_to([P, KD, hi - lo]), ALU.add).then_inc(xe_mod, 1)

            def rows_low(i):
                dve.wait_ge(xe_h, i + 1)
                nc.vector.tensor_tensor(xe_lo[:, :, :], xem[:, :, :], xe_hi[:, :, :], ALU.subtract).then_inc(xe_l, 1)

            def hidden(g, i):
                dve.wait_ge(silu_done, i * GROUPS + g + 1)
                nc.vector.tensor_tensor(hid[:, g % 2, :], sg[:, g % 2, :], bank[g % 2][0:SLOTS, GROUP:2 * GROUP], ALU.mult).then_inc(hid_done, 1)

            def hidden_low(g, i):
                dve.wait_ge(hidT_h, i * GROUPS + g + 1)
                nc.vector.tensor_tensor(hT2_lo[:, g % 2], bank[4 + g % 2][:, 0:2 * SLOTS].rearrange("p (c s) -> p c s", c=2),
                                        hT2_hi[:, g % 2], ALU.subtract).then_inc(hidT_l, 1)

            def expert(i, last):
                nc.vector.tensor_copy(gate_cur[:, :], gateT[:, bass.ds(i, 1)]).then_inc(gate_set, 1)
                low_of(2, i)
                low_of(3, i)
                low_of(4, i)
                hidden(0, i)
                for g in range(1, GROUPS):
                    if g > 1:
                        low_of(3 * g + 1, i)
                    hidden_low(g - 1, i)
                    if 3 * g + 2 < EXP_UNITS:
                        low_of(3 * g + 2, i)
                    if 3 * g + 3 < EXP_UNITS:
                        low_of(3 * g + 3, i)
                    hidden(g, i)
                    if g == 7 and not last:
                        modulate(i + 1)
                if not last:
                    rows_low(i + 1)
                hidden_low(GROUPS - 1, i)
                if not last:
                    low_of(0, i + 1)
                    low_of(1, i + 1)
                dve.wait_ge(unit_used, unit(0, i + 1))
                dve.wait_ge(gate_set, i + 1)
                dve.wait_ge(y_free, i + 1)
                for half in range(2):
                    cols = slice(half * 512, half * 512 + 512)
                    nc.vector.scalar_tensor_tensor(out=yrow[:, cols], in0=bank[2 + half][0:SLOTS, :], scalar=gate_cur[:, :],
                                                   in1=gate_f[:, cols], op0=ALU.mult, op1=ALU.mult).then_inc(y_done, 1)
                dve.wait_ge(y_done, 2 * i + 4)

            dve.sem_inc(y_done, 2)
            low_of(0, 0)
            low_of(1, 0)
            modulate(0)
            rows_low(0)
            dve.wait_ge(xn2_out, 32)
            with dve.Fori(0, EXPERTS - 1) as i:
                expert(i, False)
            expert(EXPERTS - 1, True)
            dve.wait_ge(fin_in, 16)
            for t in range(TILES):
                dve.wait_ge(f_rt, t + 1)
                step(nc.vector.reciprocal(rstd[:, t:t + 1], rstd[:, t:t + 1]))
                nc.vector.scalar_tensor_tensor(out=acc_sb[:, t, :], in0=acc_sb[:, t, :], scalar=rstd[:, t:t + 1], in1=fin_g[:, :],
                                               op0=ALU.mult, op1=ALU.mult).then_inc(f_done, 1)

        @block.tensor
        def _(pe):
            def product(out, xh, xl, wh, wl, first, last):
                nc.tensor.matmul(out, xh, wh, start=first, stop=False)
                nc.tensor.matmul(out, xh, wl, start=False, stop=False)
                return nc.tensor.matmul(out, xl, wh, start=False, stop=last)

            def split_ready(u):
                pe.wait_ge(hi_done, u + 1)
                pe.wait_ge(lo_done, u + 1)

            def parts(u, k):
                a = (u % SPLIT)
                return [w[:, a, :].rearrange("p (k n) -> p k n", k=k) for w in (w_hi, w_lo)]

            pe.wait_ge(vec_in, 16 * 7)
            pe.wait_ge(const_in, 16)
            nc.tensor.transpose(bank[7][:, 0:V_ROWS], vecs[:, :], ident[0:V_ROWS, 0:V_ROWS]).then_inc(vecT_ps, 1)
            pe.wait_ge(cond_hi, 1)
            pe.wait_ge(cond_lo, 1)

            def ada(b):
                out, u0 = ada_bank(b)[:, :], ada_unit(b)
                if b < ADA_FIRST:
                    if b >= 2:
                        pe.wait_ge(mod_row, b - 1)
                else:
                    pe.wait_ge(mod_done, b)
                for kh in range(2):
                    split_ready(u0 + kh)
                    wh, wl = parts(u0 + kh, 4)
                    for k in range(4):
                        x = cond[:, 4 * kh + k, :]
                        nc.tensor.matmul(out, x, wh[:, k, :], start=kh + k == 0, stop=False)
                        last = nc.tensor.matmul(out, x, wl[:, k, :], start=False, stop=kh + k == 4)
                    last.then_inc(unit_used, 1)

            def ada_turn(b):
                pe.wait_ge(mod_row, b + 1)
                if 1 <= b < ADA_FIRST:
                    pe.wait_ge(mod_done, b)
                for j in range(4):
                    last = nc.tensor.transpose(turn_bank(b)[:, 4 * j:4 * j + 4], modrow[:, b % 2, j * P:(j + 1) * P], ident[0:4, 0:4])
                last.then_inc(mod_ps, 1)

            for b in range(ADA_FIRST):
                ada(b)
                if b == 0:
                    pe.wait_ge(vecT_sb, 1)
                if b >= 1:
                    ada_turn(b - 1)
            ada_turn(ADA_FIRST - 1)
            pe.wait_ge(x_norm, TILES)
            for kt in range(KD + 1):
                if kt < KD:
                    if kt >= 2:
                        pe.wait_ge(hl_done, kt - 1)
                        pe.wait_ge(hc_done, kt - 1)
                    for t in range(TILES):
                        dst = bank[2 * (kt % 2)][:, t * P:(t + 1) * P] if t < T_LAT else bank[2 * (kt % 2) + 1][:, 0:P]
                        last = nc.tensor.transpose(dst, xn[:, t, kt * P:(kt + 1) * P], ident)
                    last.then_inc(xT_ps, 1)
                k = kt - 1
                if k < 0:
                    continue
                if k == 0:
                    pe.wait_ge(wza_h, 1)
                    pe.wait_ge(wza_l, 1)
                    pe.wait_ge(mod_done, ADA_FIRST)
                pe.wait_ge(h_hi, k + 1)
                pe.wait_ge(h_lo, k + 1)
                for cols, out in ((slice(0, L_LAT), bank[5][0:SLOTS, :]), (slice(L_LAT, NTOK), bank[6][0:SLOTS, 0:P])):
                    last = product(out, wza_hi[:, k, :], wza_lo[:, k, :], hT_hi[:, k, cols], hT_lo[:, k, cols], k == 0, k == KD - 1)
            last.then_inc(za_ps, 1)
            for b in range(4):
                for kh in range(2):
                    u = WIN0 + 2 * b + kh
                    split_ready(u)
                    wh, wl = parts(u, 4)
                    for t in range(TILES):
                        tok = slice(t * P, (t + 1) * P)
                        if kh == 0 and b == 0 and t < 4:
                            pe.wait_ge(hl_done, KD)
                            pe.wait_ge(hc_done, KD)
                        if kh == 0 and b > 0:
                            if t % 2 == 0:
                                pe.wait_ge(evac_act, 3 * (b - 1) + t // 2 + 1)
                            else:
                                pe.wait_ge(evac_dve, 2 * (b - 1) + t // 2 + 1)
                        for k in range(4):
                            kk = 4 * kh + k
                            last = product(bank[t][:, :], hT_hi[:, kk, tok], hT_lo[:, kk, tok], wh[:, k, :], wl[:, k, :], kk == 0, kk == KD - 1)
                        if t == TILES - 1:
                            last.then_inc(unit_used, 1)
                        elif kh == 1:
                            last.then_inc(win_ps, 1)
                        if b == 0 and kh == 0:
                            if t == 0:
                                pe.wait_ge(za_sb, 2)
                                pe.wait_ge(up_in, 64)
                                pe.wait_ge(cleared, 5)
                            if t >= 2:
                                pe.wait_ge(la_min, t - 1)
                            nc.tensor.matmul(bank[5 + t % 2][:, :], zaT[:, tok], wup[:, :], start=True, stop=True).then_inc(la_ps, 1)

            def gla_1(t):
                if t == 0:
                    pe.wait_ge(evac_act, 3 * 3 + TILES)
                    pe.wait_ge(evac_dve, 2 * 3)
                    pe.wait_ge(la_done, TILES)
                if t >= 1:
                    pe.wait_ge(g_exp, 2 * t)
                    pe.wait_ge(g_kst, t)
                for cq in range(4):
                    nc.tensor.transpose(bank[2][:, cq * P:(cq + 1) * P], proj[:, t, 0, cq * P:(cq + 1) * P], ident)
                for cc in range(4):
                    last = nc.tensor.matmul(bank[0][:, cc * P:(cc + 1) * P], la[:, t, cc * P:(cc + 1) * P], tri[cc // 2], start=True, stop=True)
                last.then_inc(g_s1, 1)

            def gla_2(t):
                s = t % 2
                pe.wait_ge(g_kst, t + 1)
                if t >= 1:
                    pe.wait_ge(g_mask, t)
                for a in range(2):
                    for h in range(HEADS):
                        hp, r = h // 2, slice(h % 2 * DK, h % 2 * DK + DK)
                        cq = 2 * a + hp
                        last = nc.tensor.matmul(bank[4 + h % 2][:, cq * P:(cq + 1) * P], kint[r, s, 2 * a + hp, :], qdec[r, t, 2 * a + hp, :], start=True, stop=True)
                last.then_inc(g_attn, 1)
                if t >= 1:
                    pe.wait_ge(g_kvs, 4 * t)
                for cc in range(4):
                    last = nc.tensor.transpose(bank[6][:, cc * P:(cc + 1) * P], kstT[:, s, cc, :], ident)
                last.then_inc(g_kstT, 1)

            def gla_3(t):
                s = t % 2
                pe.wait_ge(g_kcopy, t + 1)
                for ch in range(2):
                    rows_ = slice(ch * CHUNK, (ch + 1) * CHUNK)
                    for a in range(2):
                        for h in range(HEADS):
                            hp, par = divmod(h, 2)
                            last = nc.tensor.matmul(bank[7 - ch][par * DK:par * DK + DK, (2 * a + hp) * DV:(2 * a + hp + 1) * DV],
                                                    kst[rows_, s, 2 * a + hp, par * DK:par * DK + DK],
                                                    proj[rows_, t, 1, h * DV:(h + 1) * DV], start=True, stop=True)
                    last.then_inc(g_kv, 1)

            gla_1(0)
            for t in range(TILES):
                if t + 1 < TILES:
                    gla_1(t + 1)
                gla_2(t)
                ada(ADA_FIRST + t)
                gla_3(t)
                ada_turn(ADA_FIRST + t)
            pe.wait_ge(g_mask, TILES)
            pe.wait_ge(g_kvs, 4 * TILES)
            for t in range(TILES):
                if t >= 2:
                    pe.wait_ge(p_sb, t - 1)
                for g in range(4):
                    last = nc.tensor.matmul(bank[5 + t % 2][:, g * P:(g + 1) * P], proj[:, t, 2, g * P:(g + 1) * P],
                                            pool_mat(g, CTX if t == T_LAT else LAT), start=True, stop=True)
                last.then_inc(p_ps, 1)
            pe.wait_ge(p_sb, TILES)
            ada(9)
            pe.wait_ge(scan_done, HP)
            pe.wait_ge(mod_done, ADA_FIRST + TILES + 1)
            for t in range(TILES):
                for h in range(HEADS):
                    hp, r = h // 2, slice(h % 2 * DK, h % 2 * DK + DK)
                    cols = slice(h * DV, (h + 1) * DV)
                    out = o_bank(t, h % 2)[:, hp, :]
                    nc.tensor.matmul(out, attn[:, t, h, :], proj[:, t, 1, cols], start=True, stop=False)
                    for ch in range(2):
                        tok = slice(ch * CHUNK, (ch + 1) * CHUNK)
                        for a in range(2):
                            last = nc.tensor.matmul(out[tok, :], qdec[r, t, 2 * a + hp, tok],
                                                    S[r, state_slot(t, ch, a, True), hp, :], start=False, stop=a == 1)
                last.then_inc(o_ps, 1)
            ada_turn(9)

            def same_rows(out, chunk, s, m):
                return nc.tensor.matmul(out, modT[:, chunk, s:s + 1].broadcast_to([P, m]), ident, start=True, stop=True)

            for q in range(4):
                if q == 1:
                    pe.wait_ge(mod_done, 11)
                if q >= 2:
                    pe.wait_ge(gate_sb, q - 1)
                for j in range(4):
                    last = same_rows(bank[5 + q % 2][:, j * P:(j + 1) * P], 16 + 4 * (q % 2) + j, q // 2, P)
                last.then_inc(gate_ps, 1)
            pe.wait_ge(gate_sb, 3)
            ada(10)
            pe.wait_ge(gate_sb, 4)
            pe.wait_ge(o_n, TILES)
            for m in range(2 * HEADS):
                h = m % HEADS
                if m == HEADS:
                    ada(11)
                    ada_turn(10)
                    ada_turn(11)
                if m >= 4:
                    pe.wait_ge(m_lo, m - 3)
                if m < HEADS:
                    for t in range(TILES):
                        dst = mix_bank(m)[:, t * P:(t + 1) * P] if t < T_LAT else mix_ctx(m)
                        last = nc.tensor.transpose(dst, on[:, t, h, :], ident)
                else:
                    nc.tensor.matmul(mix_bank(m), wpool[:, h, :], pT[:, h, 0:L_LAT], start=True, stop=True)
                    last = nc.tensor.matmul(mix_ctx(m), wpool[:, h, :], pT[:, h, L_LAT:NTOK], start=True, stop=True)
                last.then_inc(m_ps, 1)
            pe.wait_ge(mod_done, ADA_BLOCKS + 1)
            for half in range(2):
                for s, lo, hi in ((LAT, 0, CAP_LAT), (CTX, CAP_LAT, SLOTS)):
                    for j in range(4):
                        last = same_rows(bank[5 + half][lo:hi, j * P:(j + 1) * P], 40 + 4 * half + j, s, hi - lo)
                last.then_inc(gate_ps, 1)
            pe.wait_ge(m_hi, 16)
            pe.wait_ge(m_lo, 16)
            for half in range(2):
                for kh in range(2):
                    u = WOUT0 + 2 * half + kh
                    split_ready(u)
                    wh, wl = parts(u, 4)
                    for t in range(TILES):
                        if half == 1 and kh == 0:
                            pe.wait_ge(wo_ev, t + 1)
                        for k in range(4):
                            kk = 4 * kh + k
                            last = product(bank[t][:, :], mix[:, t, 0, kk, :], mix[:, t, 1, kk, :], wh[:, k, :], wl[:, k, :], kk == 0, kk == KD - 1)
                        if t == TILES - 1:
                            last.then_inc(unit_used, 1)
                        elif kh == 1:
                            last.then_inc(wo_ps, 1)
            pe.wait_ge(x2_n, TILES)
            pe.wait_ge(gatef_sb, 2)
            pe.wait_ge(wo_ev, 2 * TILES)
            for k in range(KD + 1):
                if k < KD:
                    if k >= 2:
                        pe.wait_ge(r_lat, k - 1)
                        pe.wait_ge(r_ctx, k - 1)
                    for t in range(TILES):
                        dst = bank[2 * (k % 2)][:, t * P:(t + 1) * P] if t < T_LAT else bank[2 * (k % 2) + 1][:, 0:P]
                        last = nc.tensor.transpose(dst, xn2[:, t, k * P:(k + 1) * P], ident)
                    last.then_inc(r_ps, 1)
                if k >= 1:
                    q = k - 1
                    pe.wait_ge(r_lat, q + 1)
                    pe.wait_ge(r_ctx, q + 1)
                    nc.tensor.matmul(bank[5][0:EXPERTS, :], wrt[:, q, :], h2[:, q % 2, 0:L_LAT], start=q == 0, stop=q == KD - 1)
                    nc.tensor.matmul(bank[6][0:EXPERTS, 0:P], wrt[:, q, :], h2[:, q % 2, L_LAT:NTOK], start=q == 0, stop=q == KD - 1).then_inc(r_lg, 1)
            pe.wait_ge(r_lgs, 2)
            for t in range(TILES):
                last = nc.tensor.transpose(bank[7][:, t * EXPERTS:(t + 1) * EXPERTS], lgT[:, t * P:(t + 1) * P], ident[0:EXPERTS, 0:EXPERTS])
            last.then_inc(r_lt, 1)
            pe.wait_ge(r_pr, 1)
            for t in range(TILES):
                dst = bank[0][0:EXPERTS, t * P:(t + 1) * P] if t < T_LAT else bank[1][0:EXPERTS, 0:P]
                last = nc.tensor.transpose(dst, pr[:, t, :], ident)
            last.then_inc(r_prT, 1)
            pe.wait_ge(topk, 1)
            nc.tensor.transpose(bank[2][0:SLOTS, 0:EXPERTS], gv[:, :], ident[0:EXPERTS, 0:EXPERTS])
            nc.tensor.transpose(bank[2][0:SLOTS, EXPERTS:2 * EXPERTS], gif[:, :], ident[0:EXPERTS, 0:EXPERTS]).then_inc(idx_ps, 1)

            def turn_rows(i):
                pe.wait_ge(xg_in, 16 * i + 16)
                for q in range(2):
                    for k in range(4):
                        last = nc.tensor.transpose(bank[6 + q][:, k * SLOTS:(k + 1) * SLOTS], xg[:, (4 * q + k) * P:(4 * q + k + 1) * P],
                                                   ident[0:SLOTS, 0:SLOTS])
                    last.then_inc(xe_ps, 1)

            def into(kind, g, i):
                j = AT[kind, g]
                pe.wait_ge(hi_done, unit(j, i) + 1)
                pe.wait_ge(lo_done, unit(j, i) + 1)
                wh, wl = parts(j, KD)
                out = bank[g % 2][0:SLOTS, 0:GROUP] if kind == "gate" else bank[g % 2][0:SLOTS, GROUP:2 * GROUP]
                for k in range(KD):
                    last = product(out, xe_hi[:, k, :], xe_lo[:, k, :], wh[:, k, :], wl[:, k, :], k == 0, k == KD - 1)
                last.then_inc(unit_used, 1)

            def turn_hidden(g, i):
                pe.wait_ge(hid_done, i * GROUPS + g + 1)
                for q in range(2):
                    last = nc.tensor.transpose(bank[4 + g % 2][:, q * SLOTS:(q + 1) * SLOTS], hid[:, g % 2, q * P:(q + 1) * P],
                                               ident[0:SLOTS, 0:SLOTS])
                last.then_inc(hidT_ps, 1)

            def down(g, i):
                j = AT["down", g]
                pe.wait_ge(hi_done, unit(j, i) + 1)
                pe.wait_ge(lo_done, unit(j, i) + 1)
                pe.wait_ge(hidT_l, i * GROUPS + g + 1)
                if g == 0:
                    pe.wait_ge(y_done, 2 * i + 2)
                wh, wl = parts(j, 2)
                for q in range(2):
                    for half in range(2):
                        cols = slice(half * 512, half * 512 + 512)
                        last = product(bank[2 + half][0:SLOTS, :], hT2_hi[:, g % 2, q, :], hT2_lo[:, g % 2, q, :], wh[:, q, cols], wl[:, q, cols],
                                       g == 0 and q == 0, g == GROUPS - 1 and q == 1)
                last.then_inc(unit_used, 1)

            def expert(i, last):
                pe.wait_ge(xe_l, i + 1)
                into("gate", 0, i)
                into("up", 0, i)
                for g in range(1, GROUPS):
                    into("gate", g, i)
                    turn_hidden(g - 1, i)
                    into("up", g, i)
                    down(g - 1, i)
                    if g == 6 and not last:
                        turn_rows(i + 1)
                turn_hidden(GROUPS - 1, i)
                down(GROUPS - 1, i)

            turn_rows(0)
            with pe.Fori(0, EXPERTS - 1) as i:
                expert(i, False)
            expert(EXPERTS - 1, True)


_INS = ["x_prompt", "x_sample", "state_gla_fwd", "state_gla_bwd", "c", "c_ctx", "norm_mix_g", "w_ada", "b_ada", "w_in",
        "w_a_up_f", "b_a_f", "w_a_up_b", "b_a_b", "gla_norm_g", "w_pool", "pool_scale", "w_out", "norm_ffn_g",
        "w_router", "w_e_gate", "w_e_up", "w_e_down", "final_norm_g"]
_OUTS = [(1, L_CTX, D), (1, L_LAT, D), (1, 1, HEADS, DK, DV), (1, 1, HEADS, DK, DV)]


def shape_constants():
    import numpy as np

    k = np.zeros((P, K_COLS), np.float32)
    i = np.arange(P)
    same = i[:, None] // CHUNK == i[None, :] // CHUNK
    k[:, K_ID:K_ID + P] = np.eye(P)
    k[:, K_TRIF:K_TRIF + P] = same & (i[:, None] <= i[None, :])
    k[:, K_TRIB:K_TRIB + P] = same & (i[:, None] >= i[None, :])
    for g, w in enumerate(POOLS):
        for s, seg in ((LAT, GRID_W), (CTX, L_CTX)):
            start = i // seg * seg
            lo = np.maximum(i - w // 2, start)
            hi = np.minimum(i - w // 2 + w - 1, start + seg - 1)
            m = ((i[:, None] >= lo) & (i[:, None] <= hi)).astype(np.float32) / (hi - lo + 1).astype(np.float32)
            k[:, K_POOL + (2 * g + s) * P:K_POOL + (2 * g + s + 1) * P] = m - np.eye(P, dtype=np.float32)
    rows_n = L_LAT // GRID_W
    row = np.repeat(np.arange(rows_n), GRID_W).astype(np.float32)
    col = np.tile(np.arange(GRID_W), rows_n).astype(np.float32)
    quarter = D // 4
    omega = (1.0 / (10000.0 ** (np.arange(quarter, dtype=np.float32) / np.float32(quarter)))).astype(np.float32)
    er, ec = row[:, None] * omega[None, :], col[:, None] * omega[None, :]
    pos = np.concatenate([np.sin(er), np.cos(er), np.sin(ec), np.cos(ec)], axis=-1).astype(np.float32)
    return k, pos


def kernel(**inputs):
    import numpy as np
    import concourse.bacc as bacc
    from concourse.bass_utils import run_bass_kernel_spmd

    nc = bacc.Bacc("TRN2", target_bir_lowering=False, num_devices=1)
    k, pos = shape_constants()
    arrays, args = {}, []
    for name, a in [(name, np.ascontiguousarray(inputs[name])) for name in _INS] + [("consts", k), ("pos", pos)]:
        arrays[f"in_{name}"] = a
        args.append(nc.dram_tensor(f"in_{name}", a.shape, F32, kind="ExternalInput").ap())
    for i, shape in enumerate(_OUTS):
        args.append(nc.dram_tensor(f"out_{i}", shape, F32, kind="ExternalOutput").ap())
    build(nc, *args)
    r = run_bass_kernel_spmd(nc, [arrays], core_ids=[0])
    return tuple(r.results[0][f"out_{i}"] for i in range(len(_OUTS)))
```
